# Optimizing a Trainium2 kernel written in Bass

```python
import jax, jax.numpy as jnp
from jax import lax
import numpy as np

D_MODEL = 1024
BATCH = 1
SEQ = 256
DEPTH = 2
DEC_BATCH = 8
DEC_SEQ = 4
PAST_LEN = 2048
PAGE_SIZE = 128

W_A = D_MODEL // 2
CONV_A = 3
W_B = D_MODEL // 2
POOL_WINDOWS = (2, 4, 8, 16)
N_POOL_GROUPS = len(POOL_WINDOWS)
POOL_GROUP = W_B // N_POOL_GROUPS
POOL_BUF = max(POOL_WINDOWS) - 1
W_C = D_MODEL
LRU_HEADS = 8
LRU_HEAD_DIM = W_C // LRU_HEADS
CONV_C = 4
LRU_C = 8.0
W_D = D_MODEL // 2
CONV_D = 31
N_BRANCH = 4
IN_A = 3 * W_A
IN_B = W_B
IN_C = 2 * W_C
IN_D = 2 * W_D
IN_G = N_BRANCH * D_MODEL
OFF_B = IN_A
OFF_C = OFF_B + IN_B
OFF_D = OFF_C + IN_C
OFF_G = OFF_D + IN_D
IN_TOTAL = OFF_G + IN_G
PEER_HEADS = 8
N_KEYS = 128
N_EXPERTS = N_KEYS * N_KEYS
KEY_DIM = 128
PEER_TOPK = 16
PEER_BLOCK = 256
EPS = 1e-6

kernel_name = 'hybrid_conv_pool_rglru_conformer_peer_step'

def rmsnorm(x, g):
    xf = x.astype(jnp.float32)
    y = xf * lax.rsqrt(jnp.mean(xf * xf, axis=-1, keepdims=True) + EPS)
    return (y * g.astype(jnp.float32)).astype(x.dtype)

def layernorm(x, g, b):
    xf = x.astype(jnp.float32)
    mu = jnp.mean(xf, axis=-1, keepdims=True)
    xc = xf - mu
    var = jnp.mean(xc * xc, axis=-1, keepdims=True)
    return (xc * lax.rsqrt(var + EPS) * g.astype(jnp.float32) + b.astype(jnp.float32)).astype(x.dtype)

def causal_dwconv(ext, w):
    c = ext.shape[-1]
    return lax.conv_general_dilated(ext, w[:, None, :].astype(ext.dtype), window_strides=(1,), padding='VALID',
                                    dimension_numbers=('NWC', 'WIO', 'NWC'), feature_group_count=c)

def short_conv_mixer(u, buf, w_conv):
    b_gate, c_gate, xv = jnp.split(u, 3, axis=-1)
    z = c_gate * xv
    ext = jnp.concatenate([buf.astype(z.dtype), z], axis=1)
    y = b_gate * causal_dwconv(ext, w_conv)
    return y, ext[:, -(CONV_A - 1):]

def pool_mixer(u, buf, w_grp, scale, offset):
    bsz, t, _ = u.shape
    ext = jnp.concatenate([buf.astype(u.dtype), u], axis=1)
    cs = jnp.cumsum(ext.astype(jnp.float32), axis=1)
    cs = jnp.pad(cs, ((0, 0), (1, 0), (0, 0)))
    end = cs[:, POOL_BUF + 1:]
    pos = offset + jnp.arange(t)
    means = []
    for g, w in enumerate(POOL_WINDOWS):
        sl = slice(g * POOL_GROUP, (g + 1) * POOL_GROUP)
        start = cs[:, POOL_BUF + 1 - w: POOL_BUF + 1 - w + t, sl]
        cnt = jnp.minimum(pos + 1, w).astype(jnp.float32)[None, :, None]
        means.append((end[..., sl] - start) / cnt)
    mean = jnp.stack(means, axis=2)
    p = (mean - u.astype(jnp.float32).reshape(bsz, t, N_POOL_GROUPS, POOL_GROUP)).astype(u.dtype)
    y = jnp.einsum('btgc,gcd->btgd', p, w_grp).reshape(bsz, t, W_B) * scale
    return y, ext[:, -POOL_BUF:]

def rglru_mixer(u, conv_buf, h0, w_conv, b_conv, w_a, b_a, w_i, b_i, lam):
    xc, yg = jnp.split(u, 2, axis=-1)
    ext = jnp.concatenate([conv_buf.astype(xc.dtype), xc], axis=1)
    xconv = causal_dwconv(ext, w_conv) + b_conv
    bsz, t, _ = xconv.shape
    xh = xconv.reshape(bsz, t, LRU_HEADS, LRU_HEAD_DIM)
    r = jax.nn.sigmoid(jnp.einsum('bthi,hij->bthj', xh, w_a).reshape(bsz, t, W_C) + b_a)
    ig = jax.nn.sigmoid(jnp.einsum('bthi,hij->bthj', xh, w_i).reshape(bsz, t, W_C) + b_i)
    log_a = -LRU_C * r.astype(jnp.float32) * jax.nn.softplus(-lam.astype(jnp.float32))
    a = jnp.exp(log_a)
    bx = jnp.sqrt(-jnp.expm1(2.0 * log_a)) * (ig * xconv).astype(jnp.float32)

    def step(h, ab):
        a_t, b_t = ab
        h = a_t * h + b_t
        return h, h

    h_last, hs = lax.scan(step, h0.astype(jnp.float32), (jnp.swapaxes(a, 0, 1), jnp.swapaxes(bx, 0, 1)))
    hs = jnp.swapaxes(hs, 0, 1).astype(u.dtype)
    y = hs * jax.nn.gelu(yg)
    return y, ext[:, -(CONV_C - 1):], h_last.astype(h0.dtype)

def conformer_conv_mixer(u, buf, w_conv, b_conv, ln_g, ln_b):
    val, gate = jnp.split(u, 2, axis=-1)
    z = val * jax.nn.sigmoid(gate)
    ext = jnp.concatenate([buf.astype(z.dtype), z], axis=1)
    c = causal_dwconv(ext, w_conv) + b_conv
    y = jax.nn.silu(layernorm(c, ln_g, ln_b))
    return y, ext[:, -(CONV_D - 1):]

def token_mixer(xn, bufs, offset, p):
    buf_a, buf_pool, buf_c, h0, buf_d = bufs
    bsz, t, _ = xn.shape
    u = xn @ p['w_in']
    ya, sa = short_conv_mixer(u[..., :OFF_B], buf_a, p['conv_a_w'])
    yb, sb = pool_mixer(u[..., OFF_B:OFF_C], buf_pool, p['pool_w'], p['pool_scale'], offset)
    yc, sc, hc = rglru_mixer(u[..., OFF_C:OFF_D], buf_c, h0, p['conv_c_w'], p['conv_c_b'],
                             p['lru_wa'], p['lru_ba'], p['lru_wi'], p['lru_bi'], p['lru_lambda'])
    yd, sd = conformer_conv_mixer(u[..., OFF_D:OFF_G], buf_d, p['conv_d_w'], p['conv_d_b'], p['ln_d_g'], p['ln_d_b'])
    g = jax.nn.sigmoid((u[..., OFF_G:] + p['b_gate']).astype(jnp.float32)).astype(xn.dtype)
    g = g.reshape(bsz, t, N_BRANCH, D_MODEL)
    m = (g[:, :, 0] * (ya @ p['w_pa']) + g[:, :, 1] * (yb @ p['w_pb'])
         + g[:, :, 2] * (yc @ p['w_pc']) + g[:, :, 3] * (yd @ p['w_pd']))
    return m @ p['w_out'], (sa, sb, sc, hc, sd)

def peer_ffn(xn, wq, keys, u_tab, v_tab):
    bsz, t, d = xn.shape
    n = bsz * t
    blk = min(PEER_BLOCK, n)
    n_blk = -(-n // blk)
    flat = jnp.pad(xn.reshape(n, d), ((0, n_blk * blk - n), (0, 0))).reshape(n_blk, blk, d)

    def one_block(xb):
        q = (xb @ wq).reshape(blk, PEER_HEADS, 2, KEY_DIM)
        s = jnp.einsum('thcd,hcnd->thcn', q.astype(jnp.float32), keys.astype(jnp.float32))
        sv, si = lax.top_k(s, PEER_TOPK)
        cand = (sv[:, :, 0, :, None] + sv[:, :, 1, None, :]).reshape(blk, PEER_HEADS, PEER_TOPK * PEER_TOPK)
        best, pos = lax.top_k(cand, PEER_TOPK)
        i1 = jnp.take_along_axis(si[:, :, 0], pos // PEER_TOPK, axis=-1)
        i2 = jnp.take_along_axis(si[:, :, 1], pos % PEER_TOPK, axis=-1)
        expert = i1 * N_KEYS + i2
        gate = jax.nn.softmax(best, axis=-1)
        h = jnp.einsum('thkd,td->thk', u_tab[expert], xb)
        coef = (gate * jax.nn.gelu(h.astype(jnp.float32))).astype(xb.dtype)
        return jnp.einsum('thk,thkd->td', coef, v_tab[expert])

    out = lax.map(one_block, flat).reshape(n_blk * blk, d)[:n]
    return out.reshape(bsz, t, d)

def run_group(x, bufs, offset, layer_params, final_g):
    outs = ([], [], [], [], [])
    for l in range(DEPTH):
        p = {k: v[l] for k, v in layer_params.items()}
        lb = tuple(b[l] for b in bufs)
        mix, st = token_mixer(rmsnorm(x, p['norm1_g']), lb, offset, p)
        x = x + mix
        x = x + peer_ffn(rmsnorm(x, p['norm2_g']), p['peer_wq'], p['peer_keys'], p['peer_u'], p['peer_v'])
        for acc, s in zip(outs, st):
            acc.append(s)
    y = rmsnorm(x, final_g)
    return y, tuple(jnp.stack(acc) for acc in outs)

def setup_inputs(seed: int = 0) -> dict:
    key = jax.random.key(seed)
    ks = jax.random.split(key, 40)
    nrm = jax.random.normal
    f32 = jnp.float32
    a0 = jax.random.uniform(ks[20], (DEPTH, W_C), f32, 0.9, 0.999)
    s0 = a0 ** (1.0 / LRU_C)
    lam = jnp.log(s0) - jnp.log1p(-s0)
    return {
        'x_prompt': nrm(ks[0], (BATCH, SEQ, D_MODEL), f32),
        'x_sample': nrm(ks[1], (DEC_BATCH, DEC_SEQ, D_MODEL), f32),
        'state_conv_a': nrm(ks[2], (DEPTH, DEC_BATCH, CONV_A - 1, W_A), f32),
        'state_pool': nrm(ks[3], (DEPTH, DEC_BATCH, POOL_BUF, W_B), f32),
        'state_conv_c': nrm(ks[4], (DEPTH, DEC_BATCH, CONV_C - 1, W_C), f32),
        'state_lru_h': 0.5 * nrm(ks[5], (DEPTH, DEC_BATCH, W_C), f32),
        'state_conv_d': 0.5 * nrm(ks[6], (DEPTH, DEC_BATCH, CONV_D - 1, W_D), f32),
        'norm1_g': 1.0 + 0.02 * nrm(ks[7], (DEPTH, D_MODEL), f32),
        'w_in': nrm(ks[8], (DEPTH, D_MODEL, IN_TOTAL), f32) * D_MODEL ** -0.5,
        'b_gate': 0.01 * nrm(ks[9], (DEPTH, IN_G), f32),
        'conv_a_w': nrm(ks[10], (DEPTH, CONV_A, W_A), f32) * CONV_A ** -0.5,
        'pool_w': nrm(ks[11], (DEPTH, N_POOL_GROUPS, POOL_GROUP, POOL_GROUP), f32) * POOL_GROUP ** -0.5,
        'pool_scale': 1.0 + 0.02 * nrm(ks[12], (DEPTH, W_B), f32),
        'conv_c_w': nrm(ks[13], (DEPTH, CONV_C, W_C), f32) * CONV_C ** -0.5,
        'conv_c_b': 0.01 * nrm(ks[14], (DEPTH, W_C), f32),
        'lru_wa': nrm(ks[15], (DEPTH, LRU_HEADS, LRU_HEAD_DIM, LRU_HEAD_DIM), f32) * LRU_HEAD_DIM ** -0.5,
        'lru_ba': 0.01 * nrm(ks[16], (DEPTH, W_C), f32),
        'lru_wi': nrm(ks[17], (DEPTH, LRU_HEADS, LRU_HEAD_DIM, LRU_HEAD_DIM), f32) * LRU_HEAD_DIM ** -0.5,
        'lru_bi': 0.01 * nrm(ks[18], (DEPTH, W_C), f32),
        'lru_lambda': lam,
        'conv_d_w': nrm(ks[21], (DEPTH, CONV_D, W_D), f32) * CONV_D ** -0.5,
        'conv_d_b': 0.01 * nrm(ks[22], (DEPTH, W_D), f32),
        'ln_d_g': 1.0 + 0.02 * nrm(ks[23], (DEPTH, W_D), f32),
        'ln_d_b': 0.01 * nrm(ks[24], (DEPTH, W_D), f32),
        'w_pa': nrm(ks[25], (DEPTH, W_A, D_MODEL), f32) * W_A ** -0.5,
        'w_pb': nrm(ks[26], (DEPTH, W_B, D_MODEL), f32) * W_B ** -0.5,
        'w_pc': nrm(ks[27], (DEPTH, W_C, D_MODEL), f32) * W_C ** -0.5,
        'w_pd': nrm(ks[28], (DEPTH, W_D, D_MODEL), f32) * W_D ** -0.5,
        'w_out': nrm(ks[29], (DEPTH, D_MODEL, D_MODEL), f32) * D_MODEL ** -0.5,
        'norm2_g': 1.0 + 0.02 * nrm(ks[30], (DEPTH, D_MODEL), f32),
        'peer_wq': nrm(ks[31], (DEPTH, D_MODEL, PEER_HEADS * 2 * KEY_DIM), f32) * D_MODEL ** -0.5,
        'peer_keys': nrm(ks[32], (DEPTH, PEER_HEADS, 2, N_KEYS, KEY_DIM), f32) * KEY_DIM ** -0.5,
        'peer_u': nrm(ks[33], (DEPTH, N_EXPERTS, D_MODEL), f32) * D_MODEL ** -0.5,
        'peer_v': 0.35 * nrm(ks[34], (DEPTH, N_EXPERTS, D_MODEL), f32),
        'final_g': 1.0 + 0.02 * nrm(ks[35], (D_MODEL,), f32),
    }

def reference(x_prompt, x_sample, state_conv_a, state_pool, state_conv_c, state_lru_h, state_conv_d,
              norm1_g, w_in, b_gate, conv_a_w, pool_w, pool_scale, conv_c_w, conv_c_b,
              lru_wa, lru_ba, lru_wi, lru_bi, lru_lambda, conv_d_w, conv_d_b, ln_d_g, ln_d_b,
              w_pa, w_pb, w_pc, w_pd, w_out, norm2_g, peer_wq, peer_keys, peer_u, peer_v, final_g):
    layer_params = {
        'norm1_g': norm1_g, 'w_in': w_in, 'b_gate': b_gate, 'conv_a_w': conv_a_w,
        'pool_w': pool_w, 'pool_scale': pool_scale, 'conv_c_w': conv_c_w, 'conv_c_b': conv_c_b,
        'lru_wa': lru_wa, 'lru_ba': lru_ba, 'lru_wi': lru_wi, 'lru_bi': lru_bi, 'lru_lambda': lru_lambda,
        'conv_d_w': conv_d_w, 'conv_d_b': conv_d_b, 'ln_d_g': ln_d_g, 'ln_d_b': ln_d_b,
        'w_pa': w_pa, 'w_pb': w_pb, 'w_pc': w_pc, 'w_pd': w_pd, 'w_out': w_out,
        'norm2_g': norm2_g, 'peer_wq': peer_wq, 'peer_keys': peer_keys, 'peer_u': peer_u, 'peer_v': peer_v,
    }
    bp = x_prompt.shape[0]
    dt = x_prompt.dtype
    zero_bufs = (jnp.zeros((DEPTH, bp, CONV_A - 1, W_A), dt), jnp.zeros((DEPTH, bp, POOL_BUF, W_B), dt),
                 jnp.zeros((DEPTH, bp, CONV_C - 1, W_C), dt), jnp.zeros((DEPTH, bp, W_C), dt),
                 jnp.zeros((DEPTH, bp, CONV_D - 1, W_D), dt))
    y_prompt, (ca_p, pool_p, cc_p, h_p, cd_p) = run_group(x_prompt, zero_bufs, 0, layer_params, final_g)
    sample_bufs = (state_conv_a, state_pool, state_conv_c, state_lru_h, state_conv_d)
    y_sample, (ca_s, pool_s, cc_s, h_s, cd_s) = run_group(x_sample, sample_bufs, PAST_LEN, layer_params, final_g)
    return (y_prompt, y_sample, ca_p, ca_s, pool_p, pool_s, cc_p, cc_s, h_p, h_s, cd_p, cd_s)


_drawn_inputs = setup_inputs


def setup_inputs(seed=0):
    import zlib

    import numpy as np

    out = dict(_drawn_inputs(seed))
    spreads = {}
    factors = {'b_gate': 3.699,
     'lru_ba': 24.637,
     'lru_bi': 7.976,
     'ln_d_b': 3.149,
     'final_g': 8.667,
     'conv_d_b': 2.701}
    for name, (base, spread) in spreads.items():
        noise = np.random.default_rng([zlib.crc32(name.encode()), seed]).standard_normal(out[name].shape)
        drawn = base * np.exp(spread * noise) if base else spread * noise
        out[name] = __import__('jax').numpy.asarray(drawn.astype(out[name].dtype))
    for name, factor in factors.items():
        out[name] = (out[name] * factor).astype(out[name].dtype)
    return out
```

```python
from contextlib import ExitStack

import concourse.bass as bass
from concourse import mybir

F32 = mybir.dt.float32
U32 = mybir.dt.uint32
ALU = mybir.AluOpType
ACT = mybir.ActivationFunctionType
AX = mybir.AxisListType

P = 128
DM = 1024
KC = DM // P
TP, NB, TS = 256, 8, 4
T = TP + NB * TS
DEPTH = 2
EPS = 1e-6
RING = 4
W_A = W_B = W_D = DM // 2
CA = W_A // P
CC = DM // P
CONV = {"a": 3, "c": 4, "d": 31}
POOL_BUF = 15
PAD = {"a": 2, "b": POOL_BUF, "c": 3, "d": 30}
CHUNKS = {"a": CA, "b": CA, "c": CC, "d": CA}
LRU_C = 8.0
HEADS, TOPK, NKEYS = 8, 16, 128
HK = HEADS * TOPK
HC = HEADS * 2
TILES = 3
TILE_ROWS = [128, 128, 32]
NEG = -3.0e38


def row(m):
    return PAD[m] + TP + NB * (PAD[m] + TS)


def tail(m):
    return PAD[m] + NB * (PAD[m] + TS)


PARAMS = [("norm1", KC), ("norm2", KC), ("b_gate", 4 * KC), ("conv_a", 3 * CA), ("pool_scale", CA),
          ("conv_c", 4 * CC), ("conv_c_b", CC), ("ba", CC), ("bi", CC), ("lam", CC), ("conv_d", 31 * CA),
          ("conv_d_b", CA), ("ln_g", CA), ("ln_b", CA)]
PCOL = {}
_n = 0
for _name, _w in PARAMS:
    PCOL[_name] = _n
    _n += _w
NPAR = _n

SECTIONS = [("D", 2, 1, "1111"), ("B", 1, 1, "1111"), ("C", 4, 1, "1111"), ("S", 1, 1, "1110"), ("A", 3, 1, "1111"),
            ("MIXG", 8, 2, "1111"), ("MIXP", 8, 2, "1110"), ("OUT", 2, 1, "1111"), ("WQ", 4, 1, "1111"),
            ("KEYS", 1, 1, "1100"), ("U", 32, 1, "1111"), ("V", 32, 1, "1111")]


class Stream:

    def __init__(self):
        self.base, self.step, self.loads, self.loads_step = {}, {}, {}, {}
        tiles, loads = 0, [0] * RING
        for i, (name, groups, stride, mask) in enumerate(SECTIONS):
            if name == "MIXP":
                continue
            pair = [SECTIONS[i]] if name != "MIXG" else [SECTIONS[i], SECTIONS[i + 1]]
            total = [sum(p[3][s] == "1" for p in pair) for s in range(RING)]
            before = [0] * RING
            for j, (nm, _, _, mk) in enumerate(pair):
                self.base[nm] = tiles + RING * j
                self.step[nm] = RING * len(pair)
                self.loads[nm] = [loads[s] + before[s] for s in range(RING)]
                self.loads_step[nm] = total
                before = [before[s] + (mk[s] == "1") for s in range(RING)]
            tiles += groups * RING * len(pair)
            loads = [loads[s] + groups * total[s] for s in range(RING)]
        self.total = tiles

    def number(self, name, g, s):
        return self.base[name] + self.step[name] * g + s

    def landed(self, name, g, s):
        return 16 * (self.loads[name][s] + 1) + (16 * self.loads_step[name][s]) * g


STREAM = Stream()
EVAC = {"D": 0, "B": 8, "C": 12, "A": 28, "MIXG": 40, "OUT": 72, "WQ": 80, "U": 96}
UTAIL = 22


class Steps:

    def __init__(self, eng, sem):
        self.eng, self.sem, self.n, self.var = eng, sem, 0, 0

    def did(self, ins):
        ins.then_inc(self.sem, 1)
        self.n += 1

    def settle(self):
        self.eng.wait_ge(self.sem, self.n + self.var)

    def restart(self):
        self.eng.wait_ge(self.sem, self.n)
        self.eng.sem_clear(self.sem)
        self.n = 0

    def loop(self, count, body, per):
        before = self.n
        with self.eng.Fori(0, count) as i:
            self.var = i * per
            body(i)
            assert self.n == before + per, (self.n - before, per)
        self.var = 0
        self.n = before + per * count


def build(nc, x_in, params_in, final_in, pool_first, ext_in, h0_in, w_in, w_pool, w_lru, w_ab, w_c, w_d, w_out,
          w_q, w_keys, w_u, w_v, y_out, ext_out, h_out):
    with ExitStack() as ctx:
        def sb(name, shape, dt=F32):
            return ctx.enter_context(nc.sbuf_tensor(name, shape, dt))

        def sem(name):
            return ctx.enter_context(nc.semaphore(name))

        big = sb("big", [P, NKEYS * T])
        x = sb("x", [P, KC, T])
        xn = sb("xn", [P, KC, T])
        ring = [sb(f"ring{s}", [P, KC, P]) for s in range(RING)]
        par = sb("par", [P, NPAR])
        final_g = sb("final_g", [P, KC])
        first_cnt = sb("first_cnt", [P, CA, 16])
        ones = sb("ones", [P, P])
        iota = sb("iota", [P, P])
        ident = sb("ident", [P, P])
        stat = sb("stat", [P, 2, T])
        iota16 = sb("iota16", [P, TOPK])
        lru = sb("lru", [P, 8, CC])
        vals = sb("vals", [P, HC, TOPK])
        idxs = sb("idxs", [P, HC, TOPK], U32)
        idxf = sb("idxf", [P, HC, TOPK])
        best = sb("best", [P, HEADS, TOPK])
        pos = sb("pos", [P, HEADS, TOPK], U32)
        posab = sb("posab", [P, 2, HK], U32)
        posf = sb("posf", [P, 2, HK])
        left = sb("left", [P, 4, 256])
        routed = sb("routed", [P, TILES, 3, HK])
        denom = sb("denom", [P, TILES * HEADS])
        selT = sb("selT", [P, 3, T])
        h_last = sb("h_last", [P, CC, 1 + NB])
        h0 = sb("h0", [P, CC, NB])
        h0a = sb("h0a", [P, CC, NB])

        at = [0]

        def region(n):
            a = at[0]
            at[0] += n
            assert at[0] <= NKEYS * T, at[0]
            return big[:, a:a + n]

        def chunks(c):
            return region(c * T).rearrange("p (c t) -> p c t", c=c)

        ext = {m: region(CHUNKS[m] * row(m)).rearrange("p (c e) -> p c e", c=CHUNKS[m]) for m in "abcd"}
        d_val, d_gate, cd = chunks(CA), chunks(CA), chunks(CA)
        ua = chunks(3 * CA)
        xconv, yg, rg, ig, aa = chunks(CC), chunks(CC), chunks(CC), chunks(CC), chunks(CC)
        p_b, y_b, y_a = chunks(CA), chunks(CA), chunks(CA)
        merged, prod = chunks(KC), chunks(4)
        sq = xconv
        mixed = yg
        wins = [d_gate.rearrange("p c t -> p (c t)")[:, i * 512:i * 512 + row("b")] for i in range(2)]
        gates = ua[:, 0:4, :]
        rbase = UTAIL * RING * T
        s_all = big[:, rbase:rbase + TILES * HC * NKEYS].rearrange("p (t n) -> p t n", t=TILES)
        rwork = rbase + TILES * HC * NKEYS
        s_work = big[:, rwork:rwork + HC * NKEYS].rearrange("p (c n) -> p c n", c=HC)
        cand = big[:, rwork + 2048:rwork + 2 * 2048].rearrange("p (h n) -> p h n", h=HEADS)
        assert rwork + 2 * 2048 <= NKEYS * T
        eq = s_work.rearrange("p c n -> p (c n)")
        qT = big[:, 0:HC * T].rearrange("p (c t) -> p c t", c=HC)
        acts = big[:, :].rearrange("p (i t) -> p i t", i=NKEYS)
        onehot = xn[:, :, :].rearrange("p k t -> p (k t)")[:, 0:2048].rearrange("p (b w t i) -> p b w t i", b=2, w=2, t=4)

        bank = [ctx.enter_context(nc.psum_tensor(f"bank{i}", [P, 512], F32)) for i in range(8)]

        setup_loaded, setup_made = sem("setup_loaded"), sem("setup_made")
        landed = [sem(f"landed{s}") for s in range(RING)]
        tile_done = sem("tile_done")
        evacuated = sem("evacuated")
        par_in, ext_loaded, padded = sem("par_in"), sem("ext_loaded"), sem("padded")
        squared, sums, inverse, rooted, normed = (sem(n) for n in ("squared", "sums", "inverse", "rooted", "normed"))
        softplus_exp, softplus_arg, softplus_done = sem("softplus_exp"), sem("softplus_arg"), sem("softplus_done")
        d_conv, ln_sum1, ln_centred, ln_squared, ln_sum2, ln_scaled, silu_done = (
            sem(n) for n in ("d_conv", "ln_sum1", "ln_centred", "ln_squared", "ln_sum2", "ln_scaled", "silu_done"))
        pooled, extra_done, extra_out, c_conv = (sem(n) for n in ("pooled", "extra_done", "extra_out", "c_conv"))
        lru_exp, lru_ratio, lru_root, y_ready = (sem(n) for n in ("lru_exp", "lru_ratio", "lru_root", "y_ready"))
        chunk_merged, added = sem("chunk_merged"), sem("added")
        scores_done, scores_out, selected, weighed, gated = (
            sem(n) for n in ("scores_done", "scores_out", "selected", "weighed", "gated"))
        turned, turned_out, onehots, spread, spread_out, peer_done, peer_added = (
            sem(n) for n in ("turned", "turned_out", "onehots", "spread", "spread_out", "peer_done", "peer_added"))
        stored, v_step, route_step = sem("stored"), sem("v_step"), sem("route_step")
        first_sem, last_sem = landed[0], route_step

        def pcol(name, c, n=1):
            return par[:, PCOL[name] + c:PCOL[name] + c + n]

        def prompt_of(e, m, c=None):
            a = PAD[m]
            return e[:, :, a:a + TP] if c is None else e[:, c, a:a + TP]

        def samples_of(e, m, c=None, shift=0):
            w = PAD[m] + TS
            a = PAD[m] + TP
            v = (e[:, :, a:a + NB * w] if c is None else e[:, c, a:a + NB * w])
            v = v.rearrange("p c (b w) -> p c b w", b=NB) if c is None else v.rearrange("p (b w) -> p b w", b=NB)
            lo = PAD[m] - shift
            return v[:, :, :, lo:lo + TS] if c is None else v[:, :, lo:lo + TS]

        def by_seq(v):
            return v[:, TP:T].rearrange("p (b t) -> p b t", b=NB)

        def by_seq_all(v):
            return v[:, :, TP:T].rearrange("p c (b t) -> p c b t", b=NB)

        def norm_square(act, n):
            nc.scalar.activation(sq, x[:, :, :], ACT.Square).then_inc(squared, 1)

        def norm_sum(pe, n):
            pe.wait_ge(squared, n + 1)
            for k in range(KC):
                last = nc.tensor.matmul(bank[4][:, 0:T], ones[:, :], sq[:, k, :], start=(k == 0), stop=(k == KC - 1))
            last.then_inc(sums, 1)

        def norm_root(act, n):
            act.wait_ge(inverse, n + 1)
            nc.scalar.activation(stat[:, 1, :], stat[:, 0, :], ACT.Sqrt).then_inc(rooted, 1)

        def norm_apply(dve, steps, n, gain):
            dve.wait_ge(sums, n + 1)
            steps.did(nc.vector.tensor_scalar(stat[:, 0, :], bank[4][:, 0:T], 1.0 / DM, EPS, ALU.mult, ALU.add))
            steps.settle()
            nc.vector.reciprocal(stat[:, 0, :], stat[:, 0, :]).then_inc(inverse, 1)
            dve.wait_ge(rooted, n + 1)
            for k in range(KC):
                last = nc.vector.scalar_tensor_tensor(xn[:, k, :], x[:, k, :], gain[:, k:k + 1], stat[:, 1, :],
                                                      ALU.mult, ALU.mult)
            last.then_inc(normed, 1)

        with nc.Block() as block:
            @block.sync
            def _(sp):
                sp.dma_start(x[:, :, :], x_in.rearrange("p (k t) -> p k t", k=KC)).then_inc(setup_loaded, 16)
                sp.dma_start(final_g[:, :], final_in).then_inc(setup_loaded, 16)
                sp.dma_start(first_cnt[:, :, :], pool_first).then_inc(setup_loaded, 16)
                sp.wait_ge(setup_loaded, 48)

            @block.gpsimd
            def _(pool):
                nc.gpsimd.memset(ones[:, :], 1.0)
                nc.gpsimd.iota(iota[:, :], [[1, P]], base=0, channel_multiplier=0, allow_small_or_imprecise_dtypes=True)
                nc.gpsimd.iota(iota16[:, :], [[1, TOPK]], base=0, channel_multiplier=0,
                               allow_small_or_imprecise_dtypes=True)
                nc.gpsimd.memset(ident[:, :], 0.0).then_inc(setup_made, 1)
                pool.wait_ge(setup_made, 1)
                nc.gpsimd.affine_select(out=ident[:, :], in_=ident[:, :], compare_op=ALU.not_equal, fill=1.0, base=0,
                                        pattern=[[-1, P]], channel_multiplier=1).then_inc(setup_made, 1)
                pool.wait_ge(setup_made, 2)

        with nc.Fori(0, DEPTH) as layer:
            with nc.Block() as block:

                @block.sync
                def _(sp):
                    def load(name, g, s, src, width=KC, free=True):
                        if free:
                            sp.wait_ge(tile_done, STREAM.number(name, g, s) - RING + 1)
                        sp.dma_start(ring[s][:, 0:width, :], src.rearrange("p (k m) -> p k m", k=width))\
                          .then_inc(landed[s], 16)

                    for s in range(RING):
                        load("D", 0, s, w_in[layer, s], free=False)
                    for s in range(RING):
                        load("D", 1, s, w_in[layer, 4 + s])
                    for s in range(RING):
                        load("B", 0, s, w_in[layer, 8 + s])
                    with sp.Fori(0, 4) as g:
                        for s in range(RING):
                            load("C", g, s, w_in[layer, 4 * g + (12 + s)])
                    load("S", 0, 0, w_pool[layer], width=CA)
                    load("S", 0, 1, w_lru[layer, 0])
                    load("S", 0, 2, w_lru[layer, 1])
                    with sp.Fori(0, 3) as g:
                        for s in range(RING):
                            load("A", g, s, w_in[layer, 4 * g + (28 + s)])
                    with sp.Fori(0, KC) as m:
                        for s in range(RING):
                            load("MIXG", m, s, w_in[layer, 4 * m + (40 + s)])
                        load("MIXP", m, 0, w_ab[layer, m])
                        load("MIXP", m, 1, w_c[layer, m])
                        load("MIXP", m, 2, w_d[layer, m], width=CA)
                    with sp.Fori(0, 2) as g:
                        for s in range(RING):
                            load("OUT", g, s, w_out[layer, 4 * g + s])
                    with sp.Fori(0, 4) as g:
                        for s in range(RING):
                            load("WQ", g, s, w_q[layer, 4 * g + s])
                    for s in range(2):
                        load("KEYS", 0, s, w_keys[layer, s])
                    with sp.Fori(0, NKEYS // RING) as g:
                        for s in range(RING):
                            load("U", g, s, w_u[layer, 4 * g + s])
                    with sp.Fori(0, NKEYS // RING) as g:
                        for s in range(RING):
                            load("V", g, s, w_v[layer, 4 * g + s])

                @block.gpsimd
                def _(pool):
                    for m in "abcd":
                        last = nc.gpsimd.memset(ext[m][:, :, 0:PAD[m]], 0.0)
                    last.then_inc(padded, 1)

                @block.tensor
                def _(pe):
                    def tile(name, g, s, out, parts, count=1, evac=True):
                        pe.wait_ge(landed[s], STREAM.landed(name, g, s))
                        if evac and not (name == "D" and isinstance(g, int) and g == 0):
                            step = 4
                            pe.wait_ge(evacuated, EVAC[name] + step * g + s - RING + 1)
                        for k in range(len(parts)):
                            last = nc.tensor.matmul(out, ring[s][:, k, :], parts[k], start=(k == 0),
                                                    stop=(k == len(parts) - 1))
                        last.then_inc(tile_done, count)

                    xk = [xn[:, k, :] for k in range(KC)]
                    res = [bank[s][:, 0:T] for s in range(8)]
                    pe.wait_ge(par_in, 16)
                    norm_sum(pe, 0)
                    pe.wait_ge(normed, 1)
                    for g in range(2):
                        for s in range(RING):
                            tile("D", g, s, res[s], xk)
                    for s in range(RING):
                        tile("B", 0, s, res[s], xk)
                    with pe.Fori(0, 4) as g:
                        for s in range(RING):
                            tile("C", g, s, res[s], xk)
                    pe.wait_ge(d_conv, 1)
                    for k in range(CA):
                        last = nc.tensor.matmul(res[4], ones[:, :], cd[:, k, :], start=(k == 0), stop=(k == CA - 1))
                    last.then_inc(ln_sum1, 1)
                    pe.wait_ge(ln_centred, 1)
                    n = 0
                    for s, rhs, count in ((0, p_b, CA), (1, xconv, CC), (2, xconv, CC)):
                        pe.wait_ge(landed[s], STREAM.landed("S", 0, s))
                        pe.wait_ge(pooled if s == 0 else c_conv, 1)
                        for k in range(count):
                            if n >= 4:
                                pe.wait_ge(extra_out, n - 3)
                            last = nc.tensor.matmul(res[4 + n % 4], ring[s][:, k, :], rhs[:, k, :], start=True, stop=True)
                            n += 1
                            if k < count - 1:
                                last.then_inc(extra_done, 1)
                            else:
                                last.then_inc(tile_done, 2 if s == 2 else 1)
                    pe.wait_ge(ln_squared, 1)
                    pe.wait_ge(extra_out, 20)
                    for k in range(CA):
                        last = nc.tensor.matmul(res[4], ones[:, :], d_gate[:, k, :], start=(k == 0), stop=(k == CA - 1))
                    last.then_inc(ln_sum2, 1)
                    with pe.Fori(0, 3) as g:
                        for s in range(RING):
                            tile("A", g, s, res[s], xk)
                    with pe.Fori(0, KC) as m:
                        for s in range(RING):
                            tile("MIXG", m, s, res[s], xk)
                        pe.wait_ge(chunk_merged, m + 1)
                        pe.wait_ge(silu_done, 1)
                        pe.wait_ge(landed[0], STREAM.landed("MIXP", m, 0))
                        for k in range(CA):
                            nc.tensor.matmul(res[4], ring[0][:, k, :], y_a[:, k, :], start=(k == 0), stop=(k == CA - 1))
                        for k in range(CA):
                            last = nc.tensor.matmul(res[5], ring[0][:, CA + k, :], y_b[:, k, :], start=(k == 0),
                                                    stop=(k == CA - 1))
                        last.then_inc(tile_done, 1)
                        tile("MIXP", m, 1, res[6], [rg[:, k, :] for k in range(CC)], evac=False)
                        tile("MIXP", m, 2, res[7], [cd[:, k, :] for k in range(CA)], count=2, evac=False)
                    pe.wait_ge(chunk_merged, KC + 1)
                    with pe.Fori(0, 2) as g:
                        for s in range(RING):
                            tile("OUT", g, s, res[s], [merged[:, k, :] for k in range(KC)])
                    norm_sum(pe, 1)
                    pe.wait_ge(normed, 2)
                    with pe.Fori(0, 4) as g:
                        for s in range(RING):
                            tile("WQ", g, s, res[s], xk)
                    pe.wait_ge(evacuated, EVAC["WQ"] + HC)
                    for s in range(2):
                        pe.wait_ge(landed[s], STREAM.landed("KEYS", 0, s))
                    for tt in range(TILES):
                        if tt:
                            pe.wait_ge(scores_out, tt)
                        r = TILE_ROWS[tt]
                        for c in range(HC):
                            last = nc.tensor.matmul(bank[4 + c // 4][0:r, (c % 4) * P:(c % 4 + 1) * P],
                                                    qT[:, c, tt * P:tt * P + r], ring[c // 8][:, c % 8, :],
                                                    start=True, stop=True)
                        if tt < TILES - 1:
                            last.then_inc(scores_done, 1)
                    last.then_inc(tile_done, 4)
                    with pe.Fori(0, NKEYS // RING) as g:
                        for s in range(RING):
                            tile("U", g, s, res[s], xk)
                    pe.wait_ge(gated, 1)
                    for j in range(3):
                        for tt in range(TILES):
                            r = TILE_ROWS[tt]
                            last = nc.tensor.transpose(bank[4 + j][:, tt * P:tt * P + r], routed[0:r, tt, j, :],
                                                       ident[0:r, 0:r])
                    last.then_inc(turned, 1)
                    pe.wait_ge(turned_out, 1)
                    with pe.Fori(0, T // 8) as g:
                        for b in range(2):
                            pe.wait_ge(onehots, 2 * g + (b + 1))
                            pe.wait_ge(spread_out, 2 * g + (b + 1))
                            for t in range(4):
                                last = nc.tensor.matmul(bank[6 + b][:, t * P:(t + 1) * P], onehot[:, b, 0, t, :],
                                                        onehot[:, b, 1, t, :], start=True, stop=True)
                            last.then_inc(spread, 1)
                    pe.wait_ge(spread_out, T // 4 + 2)

                    def v_tile(g, s, start=False, stop=False):
                        pe.wait_ge(landed[s], STREAM.landed("V", g, s))
                        for c in range(KC):
                            last = nc.tensor.matmul(res[c], ring[s][:, c, :], acts[:, 4 * g + s, :], start=start, stop=stop)
                        last.then_inc(tile_done, 1)

                    groups = NKEYS // RING
                    for s in range(RING):
                        v_tile(0, s, start=(s == 0))
                    with pe.Fori(1, groups - 1) as g:
                        for s in range(RING):
                            v_tile(g, s)
                    for s in range(RING):
                        v_tile(groups - 1, s, stop=(s == RING - 1))

                @block.scalar
                def _(act):
                    def result(name, g, s):
                        act.wait_ge(tile_done, STREAM.number(name, g, s) + 1)

                    norm_square(act, 0)
                    act.dma_start(par[:, :], params_in[layer]).then_inc(par_in, 16)
                    for m in "dbca":
                        w = NB * (PAD[m] + TS)
                        act.dma_start(ext[m][:, :, PAD[m] + TP:PAD[m] + TP + w], ext_in[m][layer])\
                           .then_inc(ext_loaded, 16)
                    act.dma_start(h0[:, :, :], h0_in[layer]).then_inc(ext_loaded, 16)
                    norm_root(act, 0)
                    act.wait_ge(softplus_arg, 1)
                    nc.scalar.activation(lru[:, 1, :], lru[:, 0, :], ACT.Exp, scale=-1.0).then_inc(softplus_exp, 1)
                    for s in range(RING):
                        result("D", 0, s)
                        nc.scalar.activation(d_val[:, s, :], bank[s][:, 0:T], ACT.Copy).then_inc(evacuated, 1)
                    for s in range(RING):
                        result("D", 1, s)
                        nc.scalar.activation(d_gate[:, s, :], bank[s][:, 0:T], ACT.Sigmoid).then_inc(evacuated, 1)
                    act.wait_ge(ext_loaded, 16 * 5)
                    for s in range(RING):
                        result("B", 0, s)
                        nc.scalar.activation(prompt_of(ext["b"], "b", s), bank[s][:, 0:TP], ACT.Copy)
                        nc.scalar.activation(samples_of(ext["b"], "b", s), by_seq(bank[s][:, 0:T]), ACT.Copy)\
                          .then_inc(evacuated, 1)
                    for g in range(2):
                        for s in range(RING):
                            result("C", g, s)
                            c = 4 * g + s
                            nc.scalar.activation(prompt_of(ext["c"], "c", c), bank[s][:, 0:TP], ACT.Copy)
                            nc.scalar.activation(samples_of(ext["c"], "c", c), by_seq(bank[s][:, 0:T]), ACT.Copy)\
                              .then_inc(evacuated, 1)
                    for g in range(2):
                        for s in range(RING):
                            result("C", 2 + g, s)
                            nc.scalar.activation(yg[:, 4 * g + s, :], bank[s][:, 0:T], ACT.Gelu_apprx_tanh)\
                              .then_inc(evacuated, 1)
                    base = STREAM.number("S", 0, 0)
                    for n in range(20):
                        sl, k = (0, n) if n < CA else (1 + (n - CA) // CC, (n - CA) % CC)
                        last_of = [CA, CC, CC][sl] - 1
                        if k == last_of:
                            act.wait_ge(tile_done, base + sl + 1)
                        else:
                            act.wait_ge(extra_done, n + 1 - sl)
                        src = bank[4 + n % 4][:, 0:T]
                        if sl == 0:
                            ins = nc.scalar.activation(y_b[:, k, :], src, ACT.Identity, scale=pcol("pool_scale", k))
                        elif sl == 1:
                            ins = nc.scalar.activation(rg[:, k, :], src, ACT.Sigmoid, bias=pcol("ba", k))
                        else:
                            ins = nc.scalar.activation(ig[:, k, :], src, ACT.Sigmoid, bias=pcol("bi", k))
                        ins.then_inc(extra_out, 1)
                    act.wait_ge(ln_centred, 1)
                    nc.scalar.activation(d_gate, cd, ACT.Square).then_inc(ln_squared, 1)
                    act.wait_ge(softplus_done, 1)
                    act.wait_ge(extra_out, 20)
                    for c in range(CC):
                        nc.scalar.activation(aa[:, c, :], rg[:, c, :], ACT.Exp, scale=lru[:, 6, c:c + 1])
                    for c in range(CC):
                        last = nc.scalar.activation(rg[:, c, :], rg[:, c, :], ACT.Tanh, scale=lru[:, 7, c:c + 1])
                    last.then_inc(lru_exp, 1)
                    with act.Fori(0, 3) as g:
                        for s in range(RING):
                            result("A", g, s)
                            nc.scalar.activation(ua[:, 4 * g + s, :], bank[s][:, 0:T], ACT.Copy).then_inc(evacuated, 1)
                    act.wait_ge(inverse, 2)
                    nc.scalar.activation(stat[:, 1, :], stat[:, 0, :], ACT.Sqrt).then_inc(rooted, 1)
                    act.wait_ge(lru_ratio, 1)
                    nc.scalar.activation(rg, rg, ACT.Sqrt).then_inc(lru_root, 1)
                    act.wait_ge(ln_scaled, 1)
                    for c in range(CA):
                        last = nc.scalar.activation(cd[:, c, :], cd[:, c, :], ACT.Silu, bias=pcol("ln_b", c),
                                                    scale=pcol("ln_g", c))
                    last.then_inc(silu_done, 1)
                    act.wait_ge(y_ready, 2)
                    for m in "dbca":
                        act.dma_start(ext_out[m][layer], ext[m][:, :, TP:TP + tail(m)]).then_inc(stored, 16)
                    act.dma_start(h_out[layer], h_last[:, :, :]).then_inc(stored, 16)
                    with act.Fori(0, KC) as m:
                        act.wait_ge(chunk_merged, m + 1)
                        for s in range(RING):
                            result("MIXG", m, s)
                            nc.scalar.activation(gates[:, s, :], bank[s][:, 0:T], ACT.Sigmoid,
                                                 bias=par[:, bass.ds(m * 4 + (PCOL["b_gate"] + s), 1)])\
                              .then_inc(evacuated, 1)
                    with act.Fori(0, 2) as g:
                        for s in range(RING):
                            result("OUT", g, s)
                            nc.scalar.activation(mixed[:, 4 * g + s, :], bank[s][:, 0:T], ACT.Copy).then_inc(evacuated, 1)
                    act.wait_ge(added, 1)
                    norm_square(act, 1)
                    act.wait_ge(inverse, 3)
                    nc.scalar.activation(stat[:, 1, :], stat[:, 0, :], ACT.Sqrt).then_inc(rooted, 1)
                    act.wait_ge(stored, 16 * 5)
                    with act.Fori(0, 4) as g:
                        for s in range(RING):
                            result("WQ", g, s)
                            nc.scalar.activation(qT[:, 4 * g + s, :], bank[s][:, 0:T], ACT.Copy).then_inc(evacuated, 1)

                    def gelu(g):
                        for s in range(RING):
                            result("U", g, s)
                            nc.scalar.activation(acts[:, 4 * g + s, :], bank[s][:, 0:T], ACT.Gelu_apprx_tanh)\
                              .then_inc(evacuated, 1)

                    with act.Fori(0, UTAIL) as g:
                        gelu(g)
                    act.wait_ge(selected, TILES)
                    nc.scalar.activation(routed[:, :, 2, :], routed[:, :, 2, :], ACT.Exp).then_inc(weighed, 1)
                    with act.Fori(UTAIL, NKEYS // RING) as g:
                        gelu(g)

                @block.vector
                def _(dve):
                    V = nc.vector
                    steps = Steps(dve, v_step)
                    did, settle = steps.did, steps.settle

                    def conv(m, out, bias):
                        e, taps, n = ext[m], CONV[m], CHUNKS[m]
                        col = PCOL["conv_" + m]

                        def tap(j):
                            for c in range(n):
                                w = par[:, bass.ds(j * n + (col + c), 1)]
                                pr = e[:, c, bass.ds(j, TP)]
                                w4 = e[:, c, PAD[m] + TP:row(m)].rearrange("p (b w) -> p b w", b=NB)
                                sa = w4[:, :, bass.ds(j, TS)]
                                if isinstance(j, int):
                                    b = pcol(bias, c) if bias else 0.0
                                    did(V.tensor_scalar(out[:, c, 0:TP], pr, w, b, ALU.mult, ALU.add))
                                    did(V.tensor_scalar(by_seq(out[:, c, :]), sa, w, b, ALU.mult, ALU.add))
                                else:
                                    did(V.scalar_tensor_tensor(out[:, c, 0:TP], pr, w, out[:, c, 0:TP], ALU.mult, ALU.add))
                                    did(V.scalar_tensor_tensor(by_seq(out[:, c, :]), sa, w, by_seq(out[:, c, :]),
                                                               ALU.mult, ALU.add))

                        tap(0)

                        def body(j):
                            settle()
                            tap(j + 1)
                        steps.loop(taps - 1, body, 2 * n)

                    dve.wait_ge(par_in, 16)
                    did(V.tensor_scalar(lru[:, 0, :], pcol("lam", 0, CC), -1.0, None, ALU.mult))
                    settle()
                    V.tensor_tensor(lru[:, 0, :], lru[:, 0, :], pcol("lam", 0, CC), ALU.max).then_inc(softplus_arg, 1)
                    norm_apply(dve, steps, 0, par[:, PCOL["norm1"]:PCOL["norm1"] + KC])
                    dve.wait_ge(softplus_exp, 1)
                    did(V.tensor_scalar(lru[:, 2, :], lru[:, 1, :], 2.0, None, ALU.add))
                    settle()
                    did(V.reciprocal(lru[:, 2, :], lru[:, 2, :]))
                    settle()
                    did(V.tensor_tensor(lru[:, 3, :], lru[:, 1, :], lru[:, 2, :], ALU.mult))
                    settle()
                    did(V.tensor_tensor(lru[:, 4, :], lru[:, 3, :], lru[:, 3, :], ALU.mult))
                    settle()
                    did(V.tensor_scalar(lru[:, 5, :], lru[:, 4, :], 2.0 / 17, 2.0 / 15, ALU.mult, ALU.add))
                    for k in (13, 11, 9, 7, 5, 3, 1):
                        settle()
                        did(V.tensor_tensor(lru[:, 5, :], lru[:, 5, :], lru[:, 4, :], ALU.mult))
                        settle()
                        did(V.tensor_scalar(lru[:, 5, :], lru[:, 5, :], 2.0 / k, None, ALU.add))
                    settle()
                    did(V.tensor_tensor(lru[:, 5, :], lru[:, 5, :], lru[:, 3, :], ALU.mult))
                    did(V.tensor_scalar(lru[:, 2, :], pcol("lam", 0, CC), -1.0, 0.0, ALU.mult, ALU.max))
                    settle()
                    did(V.tensor_tensor(lru[:, 5, :], lru[:, 5, :], lru[:, 2, :], ALU.add))
                    settle()
                    V.tensor_scalar(lru[:, 6, :], lru[:, 5, :], -LRU_C, None, ALU.mult)
                    V.tensor_scalar(lru[:, 7, :], lru[:, 5, :], LRU_C, None, ALU.mult).then_inc(softplus_done, 1)

                    dve.wait_ge(padded, 1)
                    dve.wait_ge(ext_loaded, 16 * 5)
                    dve.wait_ge(evacuated, EVAC["D"] + 8)
                    did(V.tensor_tensor(prompt_of(ext["d"], "d"), d_val[:, :, 0:TP], d_gate[:, :, 0:TP], ALU.mult))
                    did(V.tensor_tensor(samples_of(ext["d"], "d"), by_seq_all(d_val), by_seq_all(d_gate), ALU.mult))
                    settle()
                    conv("d", cd, "conv_d_b")
                    settle()
                    V.sem_inc(d_conv, 1)

                    dve.wait_ge(evacuated, EVAC["B"] + 4)
                    for c in range(CA):
                        src, dst, valid = ext["b"][:, c, :], wins[0], 0
                        for level in range(c + 1):
                            d = 1 << level
                            valid += d
                            did(V.tensor_tensor(dst[:, valid:row("b")], src[:, valid:row("b")],
                                                src[:, valid - d:row("b") - d], ALU.add))
                            settle()
                            src, dst = dst, wins[1] if dst is wins[0] else wins[0]
                        w = 2 << c
                        a = PAD["b"]
                        win = src[:, a + TP:row("b")].rearrange("p (b w) -> p b w", b=NB)[:, :, a:a + TS]
                        did(V.scalar_tensor_tensor(p_b[:, c, 16:TP], src[:, a + 16:a + TP], 1.0 / w,
                                                   ext["b"][:, c, a + 16:a + TP], ALU.mult, ALU.subtract))
                        did(V.scalar_tensor_tensor(by_seq(p_b[:, c, :]), win, 1.0 / w, samples_of(ext["b"], "b", c),
                                                   ALU.mult, ALU.subtract))
                        did(V.tensor_tensor(p_b[:, c, 0:16], src[:, a:a + 16], first_cnt[:, c, :], ALU.mult))
                        settle()
                        did(V.tensor_tensor(p_b[:, c, 0:16], p_b[:, c, 0:16], ext["b"][:, c, a:a + 16], ALU.subtract))
                    settle()
                    V.sem_inc(pooled, 1)

                    dve.wait_ge(ln_sum1, 1)
                    did(V.tensor_scalar(stat[:, 0, :], bank[4][:, 0:T], 1.0 / W_D, None, ALU.mult))
                    settle()
                    V.tensor_tensor(cd, cd, stat[:, 0:1, :].to_broadcast([P, CA, T]), ALU.subtract).then_inc(ln_centred, 1)

                    dve.wait_ge(evacuated, EVAC["C"] + 8)
                    conv("c", xconv, "conv_c_b")
                    settle()
                    V.sem_inc(c_conv, 1)

                    dve.wait_ge(lru_exp, 1)
                    did(V.tensor_tensor(ig, ig, xconv, ALU.mult))
                    settle()
                    did(V.tensor_scalar(xconv, rg, 0.5, 0.5, ALU.mult, ALU.add))
                    settle()
                    did(V.reciprocal(xconv, xconv))
                    settle()
                    V.tensor_tensor(rg, rg, xconv, ALU.mult).then_inc(lru_ratio, 1)
                    dve.wait_ge(ln_sum2, 1)
                    did(V.tensor_scalar(stat[:, 0, :], bank[4][:, 0:T], 1.0 / W_D, EPS, ALU.mult, ALU.add))
                    settle()
                    V.reciprocal(stat[:, 0, :], stat[:, 0, :]).then_inc(inverse, 1)
                    dve.wait_ge(lru_root, 1)
                    did(V.tensor_tensor(ig, ig, rg, ALU.mult))
                    did(V.tensor_tensor(h0a[:, :, :], by_seq_all(aa)[:, :, :, 0], h0[:, :, :], ALU.mult))
                    settle()
                    did(V.tensor_tensor(by_seq_all(ig)[:, :, :, 0], by_seq_all(ig)[:, :, :, 0], h0a[:, :, :], ALU.add))
                    did(V.memset(by_seq_all(aa)[:, :, :, 0], 0.0))
                    did(V.memset(aa[:, :, 0:1], 0.0))
                    settle()
                    flat = [v.rearrange("p c t -> p (c t)") for v in (xconv, aa, ig)]
                    did(V.tensor_tensor_scan(flat[0], flat[1], flat[2], 0.0, ALU.mult, ALU.add))
                    dve.wait_ge(rooted, 2)
                    V.tensor_tensor(cd, cd, stat[:, 1:2, :].to_broadcast([P, CA, T]), ALU.mult).then_inc(ln_scaled, 1)
                    settle()
                    did(V.tensor_copy(h_last[:, :, 0:1], xconv[:, :, TP - 1:TP]))
                    did(V.tensor_copy(h_last[:, :, 1:1 + NB], by_seq_all(xconv)[:, :, :, TS - 1]))
                    V.tensor_tensor(rg, xconv, yg, ALU.mult).then_inc(y_ready, 1)

                    dve.wait_ge(evacuated, EVAC["A"] + 12)
                    gb, gc, xv = ua[:, 0:CA, :], ua[:, CA:2 * CA, :], ua[:, 2 * CA:3 * CA, :]
                    did(V.tensor_tensor(prompt_of(ext["a"], "a"), gc[:, :, 0:TP], xv[:, :, 0:TP], ALU.mult))
                    did(V.tensor_tensor(samples_of(ext["a"], "a"), by_seq_all(gc), by_seq_all(xv), ALU.mult))
                    settle()
                    conv("a", y_a, None)
                    settle()
                    V.tensor_tensor(y_a, y_a, gb, ALU.mult).then_inc(y_ready, 1)
                    dve.wait_ge(y_ready, 2)
                    V.sem_inc(chunk_merged, 1)

                    def mix(m):
                        dve.wait_ge(tile_done, STREAM.number("MIXP", m, 3) + 1)
                        dve.wait_ge(evacuated, EVAC["MIXG"] + 4 * m + 4)
                        for b in range(4):
                            did(V.tensor_tensor(prod[:, b, :], bank[4 + b][:, 0:T], gates[:, b, :], ALU.mult))
                        settle()
                        did(V.tensor_tensor(prod[:, 0:2, :], prod[:, 0:2, :], prod[:, 2:4, :], ALU.add))
                        settle()
                        V.tensor_tensor(merged[:, m, :], prod[:, 0, :], prod[:, 1, :], ALU.add).then_inc(chunk_merged, 1)
                        dve.wait_ge(chunk_merged, m + 2)
                    steps.loop(KC, mix, 5)

                    dve.wait_ge(evacuated, EVAC["OUT"] + 8)
                    V.tensor_tensor(x[:, :, :], x[:, :, :], mixed, ALU.add).then_inc(added, 1)
                    dve.wait_ge(added, 1)
                    dve.wait_ge(sums, 2)
                    did(V.tensor_scalar(stat[:, 0, :], bank[4][:, 0:T], 1.0 / DM, EPS, ALU.mult, ALU.add))
                    settle()
                    V.reciprocal(stat[:, 0, :], stat[:, 0, :]).then_inc(inverse, 1)
                    dve.wait_ge(rooted, 3)
                    g2 = PCOL["norm2"]
                    for k in range(KC):
                        last = V.scalar_tensor_tensor(xn[:, k, :], x[:, k, :], par[:, g2 + k:g2 + k + 1], stat[:, 1, :],
                                                      ALU.mult, ALU.mult)
                    last.then_inc(normed, 1)

                    dve.wait_ge(stored, 16 * 5)
                    for q in range(1, 4):
                        did(V.memset(s_all[32 * q:32 * q + 32, 2, :], 0.0))
                    for tt in range(TILES):
                        r = TILE_ROWS[tt]
                        if tt < TILES - 1:
                            dve.wait_ge(scores_done, tt + 1)
                        else:
                            dve.wait_ge(tile_done, STREAM.number("U", 0, 0))
                        for q in range(4):
                            last = V.tensor_copy(s_all[0:r, tt, q * 512:(q + 1) * 512], bank[4 + q][0:r, :])
                        last.then_inc(scores_out, 1)
                    dve.wait_ge(scores_out, TILES)

                    routing = Steps(dve, route_step)
                    did_r, settle_r = routing.did, routing.settle

                    def top16(src, values, where):
                        for r in range(4):
                            did_r(V.max(values(r)[:, 0:8], src(r)))
                        settle_r()
                        for r in range(4):
                            did_r(V.max_index(where(r)[:, 0:8], values(r)[:, 0:8], src(r)))
                        n = src(0).shape[-1]
                        for r in range(4):
                            did_r(V.match_replace(left[:, r, 0:n], values(r)[:, 0:8], src(r), NEG))
                        settle_r()
                        for r in range(4):
                            did_r(V.max(values(r)[:, 8:16], left[:, r, 0:n]))
                        settle_r()
                        for r in range(4):
                            did_r(V.max_index(where(r)[:, 8:16], values(r)[:, 8:16], left[:, r, 0:n]))
                        settle_r()

                    def route(tt):
                        did_r(V.tensor_copy(eq, s_all[:, tt, :]))
                        settle_r()
                        for q in range(HC // 4):
                            top16(lambda r: s_work[:, 4 * q + r, :], lambda r: vals[:, 4 * q + r, :],
                                  lambda r: idxs[:, 4 * q + r, :])
                        did_r(V.tensor_copy(idxf[:, :, :], idxs[:, :, :]))
                        v4 = vals[:, :, :].rearrange("p (h c) k -> p h c k", c=2)
                        first = v4[:, :, 0, :].unsqueeze(3).to_broadcast([P, HEADS, TOPK, TOPK])
                        second = v4[:, :, 1, :].unsqueeze(2).to_broadcast([P, HEADS, TOPK, TOPK])
                        did_r(V.tensor_tensor(cand.rearrange("p h (a b) -> p h a b", a=TOPK), first, second, ALU.add))
                        settle_r()
                        for q in range(HEADS // 4):
                            top16(lambda r: cand[:, 4 * q + r, :], lambda r: best[:, 4 * q + r, :],
                                  lambda r: pos[:, 4 * q + r, :])
                        pf = pos[:, :, :].rearrange("p h k -> p (h k)")
                        did_r(V.tensor_scalar(posab[:, 0, :], pf, 4, None, ALU.logical_shift_right))
                        did_r(V.tensor_scalar(posab[:, 1, :], pf, 15, None, ALU.bitwise_and))
                        settle_r()
                        did_r(V.tensor_copy(posf[:, :, :], posab[:, :, :]))
                        settle_r()
                        i4 = idxf[:, :, :].rearrange("p (h c) k -> p h c k", c=2)
                        e4 = eq.rearrange("p (h k j) -> p h k j", h=HEADS, k=TOPK)
                        e3 = eq.rearrange("p (s j) -> p s j", j=TOPK)
                        for c in range(2):
                            did_r(V.tensor_tensor(e3, posf[:, c, :].unsqueeze(2).to_broadcast([P, HK, TOPK]),
                                                iota16[:, :].unsqueeze(1).to_broadcast([P, HK, TOPK]), ALU.is_equal))
                            settle_r()
                            did_r(V.tensor_tensor(e4, e4, i4[:, :, c, :].unsqueeze(2).to_broadcast([P, HEADS, TOPK, TOPK]),
                                                ALU.mult))
                            settle_r()
                            did_r(V.tensor_reduce(routed[:, tt, c, :], e3, AX.X, ALU.add))
                            settle_r()
                        V.tensor_tensor(routed[:, tt, 2, :].rearrange("p (h k) -> p h k", h=HEADS), best[:, :, :],
                                        best[:, :, 0:1].to_broadcast([P, HEADS, TOPK]), ALU.subtract)\
                         .then_inc(selected, 1)
                        routing.restart()
                    with dve.Fori(0, TILES) as tt:
                        route(tt)
                    dve.wait_ge(weighed, 1)
                    w3 = routed[:, :, 2, :].rearrange("p t (h k) -> p t h k", h=HEADS)
                    d3 = denom[:, :].rearrange("p (t h) -> p t h", t=TILES)
                    did(V.tensor_reduce(d3, w3, AX.X, ALU.add))
                    settle()
                    did(V.reciprocal(denom[:, :], denom[:, :]))
                    settle()
                    V.tensor_tensor(w3, w3, d3.unsqueeze(3).to_broadcast([P, TILES, HEADS, TOPK]), ALU.mult)\
                     .then_inc(gated, 1)
                    dve.wait_ge(turned, 1)
                    for j in range(3):
                        last = V.tensor_copy(selT[:, j, :], bank[4 + j][:, 0:T])
                    last.then_inc(turned_out, 1)
                    dve.wait_ge(turned_out, 1)
                    dve.wait_ge(evacuated, EVAC["U"] + NKEYS)

                    def onehots_of(g, b):
                        for t in range(4):
                            c = 8 * g + (4 * b + t)
                            V.tensor_scalar(onehot[:, b, 0, t, :], iota[:, :], selT[:, 0, bass.ds(c, 1)], selT[:, 2, bass.ds(c, 1)],
                                            ALU.is_equal, ALU.mult)
                            last = V.tensor_scalar(onehot[:, b, 1, t, :], iota[:, :], selT[:, 1, bass.ds(c, 1)], None,
                                                   ALU.is_equal)
                        last.then_inc(onehots, 1)

                    def weigh(g, b):
                        a = acts[:, :, bass.ds(8 * g + 4 * b, 4)]
                        V.tensor_tensor(a, a, bank[6 + b][:, :].rearrange("p (t i) -> p i t", t=4), ALU.mult)\
                         .then_inc(spread_out, 1)

                    V.sem_inc(spread_out, 2)
                    onehots_of(0, 0)
                    onehots_of(0, 1)
                    with dve.Fori(0, T // 8 - 1) as g:
                        for b in range(2):
                            dve.wait_ge(spread, 2 * g + (b + 1))
                            weigh(g, b)
                            onehots_of(g + 1, b)
                    for b in range(2):
                        dve.wait_ge(spread, 2 * (T // 8 - 1) + b + 1)
                        weigh(T // 8 - 1, b)
                    dve.wait_ge(tile_done, STREAM.total)
                    for c in range(KC):
                        did(V.tensor_tensor(x[:, c, :], x[:, c, :], bank[c][:, 0:T], ALU.add))
                    settle()

            nc.sync.sem_clear(range(first_sem.num, last_sem.num + 1))
            nc.all_engine_barrier()

        with nc.Block() as block:
            @block.scalar
            def _(act):
                norm_square(act, 0)
                norm_root(act, 0)
                act.wait_ge(normed, 1)
                act.dma_start(y_out.rearrange("p (k t) -> p k t", k=KC), xn[:, :, :]).then_inc(stored, 16)
                act.wait_ge(stored, 16)

            @block.tensor
            def _(pe):
                norm_sum(pe, 0)

            @block.vector
            def _(dve):
                norm_apply(dve, Steps(dve, v_step), 0, final_g[:, :])


def kernel(**inputs):
    import numpy as np
    import concourse.bacc as bacc
    from concourse.bass_utils import run_bass_kernel_spmd

    a = {k: np.asarray(v) for k, v in inputs.items()}
    f32 = np.float32

    def columns(v, j=1):
        v = v.reshape(DEPTH, -1, P)
        return v.transpose(0, 2, 1)

    def gate_columns(v):
        return v.reshape(DEPTH, 4, KC, P).transpose(0, 3, 2, 1).reshape(DEPTH, P, 4 * KC)

    packs = {"norm1": columns(a["norm1_g"]), "norm2": columns(a["norm2_g"]), "b_gate": gate_columns(a["b_gate"]),
             "conv_a": columns(a["conv_a_w"]), "pool_scale": columns(a["pool_scale"]), "conv_c": columns(a["conv_c_w"]),
             "conv_c_b": columns(a["conv_c_b"]), "ba": columns(a["lru_ba"]), "bi": columns(a["lru_bi"]),
             "lam": columns(a["lru_lambda"]), "conv_d": columns(a["conv_d_w"]), "conv_d_b": columns(a["conv_d_b"]),
             "ln_g": columns(a["ln_d_g"]), "ln_b": columns(a["ln_d_b"])}
    params = np.concatenate([packs[n] for n, _ in PARAMS], axis=2)

    def tiles(w):
        l, d, n = w.shape
        return w.reshape(l, d // P, P, n // P, P).transpose(0, 3, 2, 1, 4).reshape(l, n // P, P, d)

    wt = tiles(a["w_in"])
    off_b, off_c, off_d, off_g = 12, 16, 32, 40
    order = [off_d + i for i in range(8)] + [off_b + i for i in range(4)] + [off_c + i for i in range(16)]
    order += list(range(12)) + [off_g + 8 * b + m for m in range(KC) for b in range(4)]
    w_in = wt[:, order]

    def ext_rows(s, m):
        v = s.reshape(DEPTH, NB, PAD[m], CHUNKS[m], P).transpose(0, 4, 3, 1, 2)
        out = np.zeros((DEPTH, P, CHUNKS[m], NB, PAD[m] + TS), f32)
        out[..., :PAD[m]] = v
        return out.reshape(DEPTH, P, CHUNKS[m], NB * (PAD[m] + TS))

    xt = np.concatenate([a["x_prompt"].reshape(TP, DM), a["x_sample"].reshape(NB * TS, DM)])
    arrays = {
        "x_in": xt.reshape(T, KC, P).transpose(2, 1, 0).reshape(P, KC * T),
        "params_in": params,
        "final_in": a["final_g"].reshape(KC, P).T,
        "pool_first": np.broadcast_to(np.array([[1.0 / min(t + 1, 2 << g) for t in range(16)] for g in range(CA)], f32),
                                      (P, CA, 16)),
        "ext_a": ext_rows(a["state_conv_a"], "a"), "ext_b": ext_rows(a["state_pool"], "b"),
        "ext_c": ext_rows(a["state_conv_c"], "c"), "ext_d": ext_rows(a["state_conv_d"], "d"),
        "h0_in": a["state_lru_h"].reshape(DEPTH, NB, CC, P).transpose(0, 3, 2, 1),
        "w_in_t": w_in,
        "w_pool": a["pool_w"].transpose(0, 2, 1, 3).reshape(DEPTH, P, CA * P),
        "w_lru": np.stack([a["lru_wa"].transpose(0, 2, 1, 3), a["lru_wi"].transpose(0, 2, 1, 3)], 1)
                   .reshape(DEPTH, 2, P, CC * P),
        "w_ab": np.concatenate([tiles(a["w_pa"]), tiles(a["w_pb"])], axis=3),
        "w_c": tiles(a["w_pc"]), "w_d": tiles(a["w_pd"]), "w_out_t": tiles(a["w_out"]), "w_q": tiles(a["peer_wq"]),
        "w_keys": a["peer_keys"].reshape(DEPTH, 2, 8, NKEYS, P).transpose(0, 1, 4, 2, 3).reshape(DEPTH, 2, P, 8 * P),
        "w_u": a["peer_u"].reshape(DEPTH, NKEYS, NKEYS, KC, P).transpose(0, 2, 4, 3, 1).reshape(DEPTH, NKEYS, P, DM),
        "w_v": a["peer_v"].reshape(DEPTH, NKEYS, NKEYS, DM).transpose(0, 2, 1, 3),
    }
    arrays = {k: np.ascontiguousarray(v) for k, v in arrays.items()}

    nc = bacc.Bacc("TRN2", target_bir_lowering=False, num_devices=1)

    def dram(name, shape, kind):
        return nc.dram_tensor(name, shape, F32, kind=kind).ap()

    i = {k: dram(k, v.shape, "ExternalInput") for k, v in arrays.items()}
    y = dram("y_out", (P, KC * T), "ExternalOutput")
    ext_out = {m: dram(f"ext_out_{m}", (DEPTH, P, CHUNKS[m], tail(m)), "ExternalOutput") for m in "abcd"}
    h_out = dram("h_out", (DEPTH, P, CC, 1 + NB), "ExternalOutput")
    build(nc, i["x_in"], i["params_in"], i["final_in"], i["pool_first"], {m: i[f"ext_{m}"] for m in "abcd"}, i["h0_in"],
          i["w_in_t"], i["w_pool"], i["w_lru"], i["w_ab"], i["w_c"], i["w_d"], i["w_out_t"], i["w_q"], i["w_keys"],
          i["w_u"], i["w_v"], y, ext_out, h_out)
    r = run_bass_kernel_spmd(nc, [arrays], core_ids=[0]).results[0]

    yt = r["y_out"].reshape(P, KC, T).transpose(2, 1, 0).reshape(T, DM)
    outs = [yt[:TP].reshape(1, TP, DM), yt[TP:].reshape(NB, TS, DM)]

    def states(m):
        e = r[f"ext_out_{m}"]
        p = e[..., :PAD[m]].transpose(0, 3, 2, 1).reshape(DEPTH, 1, PAD[m], CHUNKS[m] * P)
        s = e[..., PAD[m]:].reshape(DEPTH, P, CHUNKS[m], NB, PAD[m] + TS)[..., TS:]
        return [p, s.transpose(0, 3, 4, 2, 1).reshape(DEPTH, NB, PAD[m], CHUNKS[m] * P)]

    h = r["h_out"].transpose(0, 3, 2, 1).reshape(DEPTH, 1 + NB, DM)
    outs += states("a") + states("b") + states("c") + [h[:, :1], h[:, 1:]] + states("d")
    return tuple(np.ascontiguousarray(o) for o in outs)
```

```python
from contextlib import ExitStack

import concourse.bass as bass
from concourse import mybir

F32 = mybir.dt.float32
F32R = mybir.dt.float32r
U32 = mybir.dt.uint32
ALU = mybir.AluOpType
ACT = mybir.ActivationFunctionType
AX = mybir.AxisListType

P = 128
DM = 1024
KC = DM // P
TP, NB, TS = 256, 8, 4
T = TP + NB * TS
DEPTH = 2
EPS = 1e-6
RING = 4
W_A = W_B = W_D = DM // 2
CA = W_A // P
CC = DM // P
CONV = {"a": 3, "c": 4, "d": 31}
POOL_BUF = 15
PAD = {"a": 2, "b": POOL_BUF, "c": 3, "d": 30}
CHUNKS = {"a": CA, "b": CA, "c": CC, "d": CA}
LRU_C = 8.0
HEADS, TOPK, NKEYS = 8, 16, 128
HK = HEADS * TOPK
HC = HEADS * 2
TILES = 3
TILE_ROWS = [128, 128, 32]
NEG = -3.0e38


def row(m):
    return PAD[m] + TP + NB * (PAD[m] + TS)


def tail(m):
    return PAD[m] + NB * (PAD[m] + TS)


PARAMS = [("norm1", KC), ("norm2", KC), ("b_gate", 4 * KC), ("conv_a", 3 * CA), ("pool_scale", CA),
          ("conv_c", 4 * CC), ("conv_c_b", CC), ("ba", CC), ("bi", CC), ("lam", CC), ("conv_d", 31 * CA),
          ("conv_d_b", CA), ("ln_g", CA), ("ln_b", CA)]
PCOL = {}
_n = 0
for _name, _w in PARAMS:
    PCOL[_name] = _n
    _n += _w
NPAR = _n

SECTIONS = [("D", 2, 1, (8, 8, 8, 8)), ("B", 1, 1, (8, 8, 8, 8)), ("C", 4, 1, (8, 8, 8, 8)), ("S", 1, 1, (4, 8, 4, 4)),
            ("A", 3, 1, (8, 8, 8, 8)), ("MIXG", KC, 2, (8, 8, 8, 8)), ("MIXP", KC, 2, (4, 4, 8, 4)),
            ("OUT", 2, 1, (8, 8, 8, 8)), ("WQ", 4, 1, (8, 8, 8, 8)), ("KEYS", 1, 1, (4, 4, 4, 4)),
            ("U", 32, 1, (8, 8, 8, 8)), ("V", 32, 1, (8, 8, 8, 8))]
GROUPS = {name: groups for name, groups, _, _ in SECTIONS}
STRIDE = {name: stride for name, _, stride, _ in SECTIONS}
WIDTH = {name: widths for name, _, _, widths in SECTIONS}
FIRST, _n = {}, 0
for _name, _groups, _stride, _w in SECTIONS:
    if _name == "MIXP":
        FIRST[_name] = FIRST["MIXG"] + 1
        continue
    FIRST[_name] = _n
    _n += _groups * _stride
TOTAL = RING * _n
FOLLOWS = {"D": "B", "B": "C", "C": "S", "S": "A", "A": "MIXG", "MIXG": "MIXP", "MIXP": "OUT", "OUT": "WQ",
           "WQ": "KEYS", "KEYS": "U", "U": "V", "V": None}


def group(name, g):
    return STRIDE[name] * g + FIRST[name]


def number(name, g, s):
    return RING * group(name, g) + s


def landed_count(name, g):
    return 16 * group(name, g) + 16


EVAC = {"D": 0, "B": 8, "C": 12, "A": 28, "MIXG": 40, "OUT": 72, "WQ": 80, "U": 96}
UTAIL = 18
QCOLS = TILES * P


class Steps:

    def __init__(self, eng, sem):
        self.eng, self.sem, self.n, self.var = eng, sem, 0, 0

    def did(self, ins):
        ins.then_inc(self.sem, 1)
        self.n += 1

    def settle(self):
        self.eng.wait_ge(self.sem, self.n + self.var)

    def restart(self):
        self.eng.wait_ge(self.sem, self.n)
        self.eng.sem_clear(self.sem)
        self.n = 0

    def loop(self, count, body, per):
        before = self.n
        with self.eng.Fori(0, count) as i:
            self.var = i * per
            body(i)
            assert self.n == before + per, (self.n - before, per)
        self.var = 0
        self.n = before + per * count


def build(nc, x_in, params_in, final_in, pool_first, ext_in, h0_in, w_in, w_pool, w_lru, w_ab, w_c, w_d, w_out,
          w_q, w_keys, w_u, w_v, x_keep, y_out, ext_out, h_out):
    with ExitStack() as ctx:
        def sem(name):
            return ctx.enter_context(nc.semaphore(name))

        words = 53200
        start = (nc.sbuf_base + 31) // 32 * 32
        ctx.enter_context(nc.sbuf_tensor("arena", [P, words], F32))

        def place(name, offset, shape, dt=F32):
            n = 1
            for d in shape:
                n *= d
            assert offset + n <= words, name
            return nc.alloc_sbuf_tensor_at(name, [P] + list(shape), dt, offset=start + 4 * offset)

        o_x = NKEYS * T
        xh = place("xn_high", o_x, [KC, T], F32R)
        xl = place("xn_low", o_x + KC * T, [KC, T], F32R)
        o_w = o_x + 2 * KC * T
        raw = [place(f"raw{s}", o_w + s * DM, [KC, P]) for s in range(RING)]
        w_high = [place(f"w_high{s}", o_w + 4 * DM + s * 512, [4, P], F32R) for s in range(RING)]
        w_low = [place(f"w_low{s}", o_w + 6 * DM + s * 512, [4, P], F32R) for s in range(RING)]
        cursor = [o_w + 8 * DM]

        def keep(name, shape, dt=F32):
            n = 1
            for d in shape:
                n *= d
            at = cursor[0]
            cursor[0] += (n + 7) // 8 * 8
            return place(name, at, shape, dt)

        par = keep("par", [NPAR])
        final_g = keep("final_g", [KC])
        first_cnt = keep("first_cnt", [CA, 16])
        ones = keep("ones", [P])
        iota = keep("iota", [P])
        ident = keep("ident", [P])
        iota16 = keep("iota16", [TOPK])
        routed = keep("routed", [TILES, 3, HK])
        denom = keep("denom", [TILES * HEADS])
        selT = keep("selT", [3, T])

        offs, at = {}, 0
        for m in "abcd":
            offs["ext_" + m] = at
            at += (CHUNKS[m] * row(m) + 7) // 8 * 8
        for name, c in (("d_val", CA), ("d_gate", CA), ("cd", CA), ("ua", 3 * CA), ("xconv", CC), ("yg", CC), ("rg", CC),
                        ("ig", CC), ("aa", CC), ("p_b", CA), ("y_a", CA), ("yb_high", CA), ("yb_low", CA), ("prod", 4), ("gates", 4)):
            offs[name] = at
            at += c * T
        o_stat = at
        o_res = NKEYS * T - KC * T
        assert o_stat + 2 * T + 200 + 8 * CC <= o_res
        ext = {m: place("ext_" + m, offs["ext_" + m], [CHUNKS[m], row(m)]) for m in "abcd"}

        def over(name, slot, c, dt=F32, skip=0):
            return place(name, offs[slot] + skip * T, [c, T], dt)[:, :, :]

        d_val, d_gate, cd = over("d_val", "d_val", CA), over("d_gate", "d_gate", CA), over("cd", "cd", CA)
        ua = over("ua", "ua", 3 * CA)
        xconv, yg, rg, ig, aa = (over(n, n, CC) for n in ("xconv", "yg", "rg", "ig", "aa"))
        p_b, y_a, prod = over("p_b", "p_b", CA), over("y_a", "y_a", CA), over("prod", "prod", 4)
        y_b = over("y_b", "p_b", CA)
        wins = [place(f"win{i}", offs["d_gate"] + i * 512, [row("b")])[:, :] for i in range(2)]
        gates = over("gates", "gates", 4)
        sq = over("sq", "ig", KC)
        xnf = over("xnf", "aa", KC)
        mixed = over("mixed", "yg", KC)
        pair = {"p_b": (over("pb_high", "prod", CA, F32R), over("pb_low", "y_a", CA, F32R)),
                "xconv": (over("xc_high", "aa", CC, F32R), over("xc_low", "ua", CC, F32R)),
                "a": (over("ya_high", "ua", CA, F32R, CA), over("ya_low", "ua", CA, F32R, 2 * CA)),
                "b": (over("yb_high", "yb_high", CA, F32R), over("yb_low", "yb_low", CA, F32R)),
                "c": (over("yc_high", "aa", CC, F32R), over("yc_low", "ig", CC, F32R)),
                "d": (over("yd_high", "d_val", CA, F32R), over("yd_low", "d_gate", CA, F32R)),
                "merged": (over("merged_high", "xconv", KC, F32R), over("merged_low", "rg", KC, F32R)),
                "x": (xh[:, :, :], xl[:, :, :])}
        stat = place("stat", o_stat, [2, T])
        h_last = place("h_last", o_stat + 2 * T, [CC, 1 + NB])
        h0 = place("h0", o_stat + 2 * T + 72, [CC, NB])
        h0a = place("h0a", o_stat + 2 * T + 136, [CC, NB])
        lru = place("lru", o_stat + 2 * T + 200, [8, CC])
        x = place("x", o_res, [KC, T])
        x_back = place("x_back", 0, [KC, T])
        q_high = place("q_hi", 0, [HC, QCOLS], F32R)
        q_low = place("q_lo", HC * QCOLS, [HC, QCOLS], F32R)
        acts = place("acts", 0, [NKEYS, T])
        o_r = UTAIL * RING * T
        s_all = place("s_all", o_r, [TILES, HC * NKEYS])
        eq = place("eq", o_r + 6144, [HK * TOPK])[:, :]
        s_work = eq.rearrange("p (c i) -> p c i", c=HC)
        cand = place("cand", o_r + 8192, [HEADS, 256])
        vals = place("vals", o_r + 10240, [HC, TOPK])
        idxs = place("idxs", o_r + 10496, [HC, TOPK], U32)
        idxf = place("idxf", o_r + 10752, [HC, TOPK])
        best = place("best", o_r + 11008, [HEADS, TOPK])
        pos = place("pos", o_r + 11136, [HEADS, TOPK], U32)
        posab = place("posab", o_r + 11264, [2, HK], U32)
        posf = place("posf", o_r + 11520, [2, HK])
        left = place("left", o_r + 11776, [4, 256])
        assert o_r + 12800 <= o_res
        onehot = [raw[2 + b][:, :, :].rearrange("p (w t) i -> p w t i", w=2) for b in range(2)]
        c_high = place("c_hi", o_x + KC * T, [2, T], F32R)
        c_low = place("c_lo", o_x + KC * T + 2 * T, [2, T], F32R)

        bank = [ctx.enter_context(nc.psum_tensor(f"bank{i}", [P, 512], F32)) for i in range(8)]

        setup_loaded, setup_made = sem("setup_loaded"), sem("setup_made")
        landed = [sem(f"landed{s}") for s in range(RING)]
        gates_free, lru_a = sem("gates_free"), sem("lru_a")
        high_done, low_done = sem("high_done"), sem("low_done")
        half_done = sem("half_done")
        evacuated = sem("evacuated")
        x_raw, x_high, x_saved, x_loaded = (sem(n) for n in ("x_raw", "x_high", "x_saved", "x_loaded"))
        q_high_out, c_high_out, c_low_out = (sem(n) for n in ("q_high_out", "c_high_out", "c_low_out"))
        par_in, ext_loaded, padded = sem("par_in"), sem("ext_loaded"), sem("padded")
        squared, sums, inverse, rooted, normed = (sem(n) for n in ("squared", "sums", "inverse", "rooted", "normed"))
        softplus_exp, softplus_arg, softplus_done = sem("softplus_exp"), sem("softplus_arg"), sem("softplus_done")
        d_conv, ln_sum1, ln_centred, ln_squared, ln_sum2, ln_scaled, silu_done = (
            sem(n) for n in ("d_conv", "ln_sum1", "ln_centred", "ln_squared", "ln_sum2", "ln_scaled", "silu_done"))
        pooled, extra_done, extra_out, c_conv = (sem(n) for n in ("pooled", "extra_done", "extra_out", "c_conv"))
        lru_exp, lru_ratio, lru_root, y_ready = (sem(n) for n in ("lru_exp", "lru_ratio", "lru_root", "y_ready"))
        chunk_merged, added = sem("chunk_merged"), sem("added")
        scores_done, scores_out, selected, weighed, gated = (
            sem(n) for n in ("scores_done", "scores_out", "selected", "weighed", "gated"))
        turned, turned_out, onehots, spread, spread_out, peer_done, peer_added = (
            sem(n) for n in ("turned", "turned_out", "onehots", "spread", "spread_out", "peer_done", "peer_added"))
        stored, v_step, route_step = sem("stored"), sem("v_step"), sem("route_step")
        first_sem, last_sem = landed[0], route_step

        def pcol(name, c, n=1):
            return par[:, PCOL[name] + c:PCOL[name] + c + n]

        def prompt_of(e, m, c=None):
            a = PAD[m]
            return e[:, :, a:a + TP] if c is None else e[:, c, a:a + TP]

        def samples_of(e, m, c=None, shift=0):
            w = PAD[m] + TS
            a = PAD[m] + TP
            v = (e[:, :, a:a + NB * w] if c is None else e[:, c, a:a + NB * w])
            v = v.rearrange("p c (b w) -> p c b w", b=NB) if c is None else v.rearrange("p (b w) -> p b w", b=NB)
            lo = PAD[m] - shift
            return v[:, :, :, lo:lo + TS] if c is None else v[:, :, lo:lo + TS]

        def by_seq(v):
            return v[:, TP:T].rearrange("p (b t) -> p b t", b=NB)

        def by_seq_all(v):
            return v[:, :, TP:T].rearrange("p c (b t) -> p c b t", b=NB)

        def norm_square(act):
            nc.scalar.activation(sq, x[:, :, :], ACT.Square).then_inc(squared, 1)

        def norm_sum(pe, n):
            pe.wait_ge(squared, n + 1)
            for k in range(KC):
                last = nc.tensor.matmul(bank[4][:, 0:T], ones[:, :], sq[:, k, :], start=(k == 0), stop=(k == KC - 1))
            last.then_inc(sums, 1)

        def root(act, n):
            act.wait_ge(inverse, n + 1)
            nc.scalar.activation(stat[:, 1, :], stat[:, 0, :], ACT.Sqrt).then_inc(rooted, 1)

        def norm_scale(dve, steps, n, roots, gain):
            dve.wait_ge(sums, n + 1)
            steps.did(nc.vector.tensor_scalar(stat[:, 0, :], bank[4][:, 0:T], 1.0 / DM, EPS, ALU.mult, ALU.add))
            steps.settle()
            nc.vector.reciprocal(stat[:, 0, :], stat[:, 0, :]).then_inc(inverse, 1)
            dve.wait_ge(rooted, roots)
            for k in range(KC):
                nc.vector.scalar_tensor_tensor(xnf[:, k, :], x[:, k, :], gain[:, k:k + 1], stat[:, 1, :],
                                               ALU.mult, ALU.mult).then_inc(x_raw, 1)

        def norm_high(act, n):
            for k in range(KC):
                act.wait_ge(x_raw, KC * n + k + 1)
                nc.scalar.activation(xh[:, k, :], xnf[:, k, :], ACT.Copy).then_inc(x_high, 1)

        def norm_low(dve, n):
            for k in range(KC):
                dve.wait_ge(x_high, KC * n + k + 1)
                nc.vector.tensor_tensor(xl[:, k, :], xnf[:, k, :], xh[:, k, :].bitcast(F32), ALU.subtract)\
                  .then_inc(normed, 1)

        with nc.Block() as block:
            @block.sync
            def _(sp):
                sp.dma_start(x[:, :, :], x_in.rearrange("p (k t) -> p k t", k=KC)).then_inc(setup_loaded, 16)
                sp.dma_start(final_g[:, :], final_in).then_inc(setup_loaded, 16)
                sp.dma_start(first_cnt[:, :, :], pool_first).then_inc(setup_loaded, 16)
                sp.wait_ge(setup_loaded, 48)

            @block.gpsimd
            def _(pool):
                nc.gpsimd.memset(ones[:, :], 1.0)
                nc.gpsimd.iota(iota[:, :], [[1, P]], base=0, channel_multiplier=0, allow_small_or_imprecise_dtypes=True)
                nc.gpsimd.iota(iota16[:, :], [[1, TOPK]], base=0, channel_multiplier=0,
                               allow_small_or_imprecise_dtypes=True)
                nc.gpsimd.memset(ident[:, :], 0.0).then_inc(setup_made, 1)
                pool.wait_ge(setup_made, 1)
                nc.gpsimd.affine_select(out=ident[:, :], in_=ident[:, :], compare_op=ALU.not_equal, fill=1.0, base=0,
                                        pattern=[[-1, P]], channel_multiplier=1).then_inc(setup_made, 1)
                pool.wait_ge(setup_made, 2)

        with nc.Fori(0, DEPTH) as layer:
            with nc.Block() as block:

                @block.sync
                def _(sp):
                    def load(name, g, s, src, free=True):
                        if free:
                            sp.wait_ge(low_done, 2 * number(name, g, s) - 2 * RING + 2)
                        width = WIDTH[name][s]
                        sp.dma_start(raw[s][:, 0:width, :], src.rearrange("p (k m) -> p k m", k=width))\
                          .then_inc(landed[s], 16)

                    for s in range(RING):
                        load("D", 0, s, w_in[layer, s], free=False)
                    with sp.Fori(1, 7) as g:
                        for s in range(RING):
                            load("D", g, s, w_in[layer, 4 * g + s])
                    load("S", 0, 0, w_pool[layer])
                    load("S", 0, 1, w_lru[layer, 0])
                    for half in range(2):
                        load("S", 0, 2 + half, w_lru[layer, 1, :, 512 * half:512 * half + 512])
                    with sp.Fori(0, 3) as g:
                        for s in range(RING):
                            load("A", g, s, w_in[layer, 4 * g + (28 + s)])
                    with sp.Fori(0, KC) as m:
                        for s in range(RING):
                            load("MIXG", m, s, w_in[layer, 4 * m + (40 + s)])
                        load("MIXP", m, 0, w_ab[layer, 0, m])
                        load("MIXP", m, 1, w_ab[layer, 1, m])
                        load("MIXP", m, 2, w_c[layer, m])
                        load("MIXP", m, 3, w_d[layer, m])
                    with sp.Fori(0, 2) as g:
                        for s in range(RING):
                            load("OUT", g, s, w_out[layer, 4 * g + s])
                    with sp.Fori(0, 4) as g:
                        for s in range(RING):
                            load("WQ", g, s, w_q[layer, 4 * g + s])
                    for s in range(RING):
                        load("KEYS", 0, s, w_keys[layer, s])
                    with sp.Fori(0, GROUPS["U"]) as g:
                        for s in range(RING):
                            load("U", g, s, w_u[layer, 4 * g + s])
                    load("V", 0, 0, w_v[layer, 0])
                    load("V", 0, 1, w_v[layer, 1])
                    sp.wait_ge(spread_out, T // 4 + 2)
                    load("V", 0, 2, w_v[layer, 2])
                    load("V", 0, 3, w_v[layer, 3])
                    with sp.Fori(1, 4) as g:
                        for s in range(RING):
                            load("V", g, s, w_v[layer, 4 * g + s])
                    sp.wait_ge(x_saved, 16)
                    sp.wait_ge(half_done, 2 * number("V", 2, 0))
                    sp.dma_start(x_back[:, :, :], x_keep.rearrange("p (k t) -> p k t", k=KC)).then_inc(x_loaded, 16)
                    with sp.Fori(4, GROUPS["V"]) as g:
                        for s in range(RING):
                            load("V", g, s, w_v[layer, 4 * g + s])

                @block.gpsimd
                def _(pool):
                    for m in "abcd":
                        last = nc.gpsimd.memset(ext[m][:, :, 0:PAD[m]], 0.0)
                    last.then_inc(padded, 1)

                    def low(grp, s, width=8):
                        for half in range(width // 4):
                            n = 2 if width == 4 else 1
                            pool.wait_ge(high_done, 8 * grp + (2 * s + half + n))
                            slot = 2 * (s % 2) + half
                            nc.gpsimd.tensor_tensor(w_low[slot][:, :, :], raw[s][:, 4 * half:4 * half + 4, :],
                                                    w_high[slot][:, :, :].bitcast(F32), ALU.subtract)\
                              .then_inc(low_done, n)

                    def full_groups(first, count):
                        with pool.Fori(0, count) as g:
                            for s in range(RING):
                                low(g + first, s)

                    def narrow_group(name, g):
                        for s in range(RING):
                            low(group(name, g), s, WIDTH[name][s])

                    full_groups(0, 7)
                    narrow_group("S", 0)
                    full_groups(FIRST["A"], 3)
                    with pool.Fori(0, KC) as m:
                        narrow_group("MIXG", m)
                        narrow_group("MIXP", m)
                    full_groups(FIRST["OUT"], 6)
                    narrow_group("KEYS", 0)
                    full_groups(FIRST["U"], 64)

                @block.tensor
                def _(pe):
                    res = [bank[s][:, 0:T] for s in range(8)]

                    def product(out, high, low, moving, start, stop):
                        m_high, m_low = moving
                        nc.tensor.matmul(out, high, m_high, start=start, stop=False)
                        nc.tensor.matmul(out, high, m_low, start=False, stop=False)
                        return nc.tensor.matmul(out, low, m_high, start=False, stop=stop)

                    def halves(name, g, s):
                        width = WIDTH[name][s]
                        for half in range(width // 4):
                            n = 2 if width == 4 else 1
                            pe.wait_ge(low_done, 2 * number(name, g, s) + (half + n))
                            slot = 2 * (s % 2) + half
                            yield 4 * half, w_high[slot], w_low[slot], n

                    def tile(name, g, s, out, src, evac=True, first=None):
                        if evac and not (name == "D" and g == 0):
                            pe.wait_ge(evacuated, RING * g + (EVAC[name] + s - RING + 1))
                        width = WIDTH[name][s]
                        high, low = pair[src]
                        for k0, wh, wl, n in halves(name, g, s):
                            for k in range(4):
                                if first is not None:
                                    pe.wait_ge(normed, KC * first + k0 + k + 1)
                                last = product(out, wh[:, k, :], wl[:, k, :], (high[:, k0 + k, :], low[:, k0 + k, :]),
                                               k0 + k == 0, k0 + k == width - 1)
                            last.then_inc(half_done, n)

                    norm_sum(pe, 0)
                    for s in range(RING):
                        tile("D", 0, s, res[s], "x", first=0)
                    for s in range(RING):
                        tile("D", 1, s, res[s], "x")
                    for s in range(RING):
                        tile("B", 0, s, res[s], "x")
                    with pe.Fori(0, 4) as g:
                        for s in range(RING):
                            tile("C", g, s, res[s], "x")
                    pe.wait_ge(d_conv, 1)
                    for k in range(CA):
                        last = nc.tensor.matmul(res[4], ones[:, :], cd[:, k, :], start=(k == 0), stop=(k == CA - 1))
                    last.then_inc(ln_sum1, 1)
                    pe.wait_ge(ln_centred, 1)
                    n = 0
                    for s, src in enumerate(("p_b", "xconv", "xconv", "xconv")):
                        pe.wait_ge(pooled if s == 0 else c_conv, 1)
                        high, low = pair[src]
                        for k0, wh, wl, count in halves("S", 0, s):
                            k0 += 4 * (s == 3)
                            for k in range(4):
                                if n >= 4:
                                    pe.wait_ge(extra_out, n - 3)
                                last = product(res[4 + n % 4], wh[:, k, :], wl[:, k, :],
                                               (high[:, k0 + k, :], low[:, k0 + k, :]), True, True)
                                n += 1
                                last.then_inc(*((extra_done, 1) if k < 3 else (half_done, count)))
                    pe.wait_ge(ln_squared, 1)
                    pe.wait_ge(extra_out, 20)
                    for k in range(CA):
                        last = nc.tensor.matmul(res[4], ones[:, :], d_gate[:, k, :], start=(k == 0), stop=(k == CA - 1))
                    last.then_inc(ln_sum2, 1)
                    with pe.Fori(0, 3) as g:
                        for s in range(RING):
                            tile("A", g, s, res[s], "x")
                    with pe.Fori(0, KC) as m:
                        for s in range(RING):
                            tile("MIXG", m, s, res[s], "x")
                        pe.wait_ge(chunk_merged, m + 1)
                        for s, src in enumerate("abcd"):
                            tile("MIXP", m, s, res[4 + s], src, evac=False)
                    pe.wait_ge(chunk_merged, KC + 1)
                    with pe.Fori(0, 2) as g:
                        for s in range(RING):
                            tile("OUT", g, s, res[s], "merged")
                    norm_sum(pe, 1)
                    for s in range(RING):
                        tile("WQ", 0, s, res[s], "x", first=1)
                    with pe.Fori(1, 4) as g:
                        for s in range(RING):
                            tile("WQ", g, s, res[s], "x")
                    pe.wait_ge(evacuated, EVAC["WQ"] + HC)
                    n = 0
                    for s in range(RING):
                        for _, wh, wl, count in halves("KEYS", 0, s):
                            for tt in range(TILES):
                                if n >= 4:
                                    pe.wait_ge(scores_out, n - 3)
                                for c in range(4):
                                    out = bank[4 + n % 4][:, c * P:(c + 1) * P]
                                    qh = q_high[:, 4 * s + c, tt * P:(tt + 1) * P]
                                    ql = q_low[:, 4 * s + c, tt * P:(tt + 1) * P]
                                    last = product(out, qh, ql, (wh[:, c, :], wl[:, c, :]), True, True)
                                n += 1
                                last.then_inc(*((scores_done, 1) if tt < TILES - 1 else (half_done, count)))
                    with pe.Fori(0, GROUPS["U"]) as g:
                        for s in range(RING):
                            tile("U", g, s, res[s], "x")
                    pe.wait_ge(gated, 1)
                    for j in range(3):
                        for tt in range(TILES):
                            r = TILE_ROWS[tt]
                            last = nc.tensor.transpose(bank[4 + j][:, tt * P:tt * P + r], routed[0:r, tt, j, :],
                                                       ident[0:r, 0:r])
                    last.then_inc(turned, 1)
                    pe.wait_ge(turned_out, 1)
                    with pe.Fori(0, T // 8) as g:
                        for b in range(2):
                            pe.wait_ge(onehots, 2 * g + (b + 1))
                            pe.wait_ge(spread_out, 2 * g + (b + 1))
                            for t in range(4):
                                last = nc.tensor.matmul(bank[6 + b][:, t * P:(t + 1) * P], onehot[b][:, 0, t, :],
                                                        onehot[b][:, 1, t, :], start=True, stop=True)
                            last.then_inc(spread, 1)
                    pe.wait_ge(spread_out, T // 4 + 2)

                    def v_tile(g, s, start=False, stop=False):
                        pe.wait_ge(c_low_out, RING * g + (s + 1))
                        moving = (c_high[:, s % 2, :], c_low[:, s % 2, :])
                        for c0, wh, wl, n in halves("V", g, s):
                            for c in range(4):
                                last = product(res[c0 + c], wh[:, c, :], wl[:, c, :], moving, start, stop)
                            last.then_inc(half_done, n)

                    groups = GROUPS["V"]
                    for s in range(RING):
                        v_tile(0, s, start=(s == 0))
                    with pe.Fori(1, groups - 1) as g:
                        for s in range(RING):
                            v_tile(g, s)
                    for s in range(RING):
                        v_tile(groups - 1, s, stop=(s == RING - 1))

                @block.scalar
                def _(act):
                    A = nc.scalar.activation

                    def split(grp, s, width=8):
                        act.wait_ge(landed[s], 16 * grp + 16)
                        for half in range(width // 4):
                            if not (isinstance(grp, int) and RING * grp + s < 2):
                                act.wait_ge(half_done, 8 * grp + (2 * s + half - 3))
                            A(w_high[2 * (s % 2) + half][:, :, :], raw[s][:, 4 * half:4 * half + 4, :], ACT.Copy)\
                                .then_inc(high_done, 2 if width == 4 else 1)

                    def ahead(name, g, s, following=(8, 8)):
                        if s < 2:
                            split(group(name, g), s + 2, WIDTH[name][s + 2])
                        else:
                            split(group(name, g) + 1, s - 2, following[s - 2])

                    def step(name, g, s, out, func=ACT.Copy, following=(8, 8), signal=evacuated, **kw):
                        ahead(name, g, s, following)
                        act.wait_ge(half_done, 2 * number(name, g, s) + 2)
                        A(out, bank[s][:, 0:T], func, **kw).then_inc(signal, 1)

                    norm_square(act)
                    act.dma_start(par[:, :], params_in[layer]).then_inc(par_in, 16)
                    for m in "dbca":
                        w = NB * (PAD[m] + TS)
                        act.dma_start(ext[m][:, :, PAD[m] + TP:PAD[m] + TP + w], ext_in[m][layer])\
                           .then_inc(ext_loaded, 16)
                    act.dma_start(h0[:, :, :], h0_in[layer]).then_inc(ext_loaded, 16)
                    split(0, 0)
                    split(0, 1)
                    root(act, 0)
                    norm_high(act, 0)
                    act.wait_ge(softplus_arg, 1)
                    A(lru[:, 1, :], lru[:, 0, :], ACT.Exp, scale=-1.0).then_inc(softplus_exp, 1)
                    for s in range(RING):
                        step("D", 0, s, d_val[:, s, :])
                    for s in range(RING):
                        step("D", 1, s, d_gate[:, s, :], ACT.Sigmoid)
                    act.wait_ge(ext_loaded, 16 * 5)

                    def into_ext(m, name, g, s, c):
                        ahead(name, g, s)
                        act.wait_ge(half_done, 2 * number(name, g, s) + 2)
                        A(prompt_of(ext[m], m, c), bank[s][:, 0:TP], ACT.Copy)
                        A(samples_of(ext[m], m, c), by_seq(bank[s][:, 0:T]), ACT.Copy).then_inc(evacuated, 1)

                    for s in range(RING):
                        into_ext("b", "B", 0, s, s)
                    for g in range(2):
                        for s in range(RING):
                            into_ext("c", "C", g, s, 4 * g + s)
                    for g in range(2):
                        for s in range(RING):
                            step("C", 2 + g, s, yg[:, 4 * g + s, :], ACT.Gelu_apprx_tanh,
                                 following=(8, 8) if g == 0 else WIDTH["S"])
                    n = 0
                    for s in range(RING):
                        for half in range(WIDTH["S"][s] // 4):
                            for k in range(4):
                                if k < 3:
                                    act.wait_ge(extra_done, n - n // 4 + 1)
                                else:
                                    act.wait_ge(half_done, 2 * number("S", 0, s) + (half + 1 if WIDTH["S"][s] == 8 else 2))
                                src = bank[4 + n % 4][:, 0:T]
                                c = 4 * half + k + 4 * (s == 3)
                                if s == 0:
                                    ins = A(y_b[:, c, :], src, ACT.Identity, scale=pcol("pool_scale", c))
                                elif s == 1:
                                    ins = A(rg[:, c, :], src, ACT.Sigmoid, bias=pcol("ba", c))
                                else:
                                    ins = A(ig[:, c, :], src, ACT.Sigmoid, bias=pcol("bi", c))
                                ins.then_inc(extra_out, 1)
                                n += 1
                        ahead("S", 0, s)
                    act.wait_ge(ln_centred, 1)
                    A(d_gate, cd, ACT.Square).then_inc(ln_squared, 1)
                    act.wait_ge(softplus_done, 1)
                    act.wait_ge(extra_out, 20)
                    for c in range(CC):
                        A(aa[:, c, :], rg[:, c, :], ACT.Exp, scale=lru[:, 6, c:c + 1]).then_inc(lru_a, 1)
                    act.wait_ge(lru_a, CC)
                    for c in range(CC):
                        last = A(rg[:, c, :], rg[:, c, :], ACT.Tanh, scale=lru[:, 7, c:c + 1])
                    last.then_inc(lru_exp, 1)
                    for g in range(3):
                        for s in range(RING):
                            step("A", g, s, ua[:, 4 * g + s, :])
                        if g == 0:
                            act.wait_ge(lru_ratio, 1)
                            A(rg, rg, ACT.Sqrt).then_inc(lru_root, 1)
                            root(act, 1)
                        if g == 1:
                            act.wait_ge(ln_scaled, 1)
                            for c in range(CA):
                                last = A(cd[:, c, :], cd[:, c, :], ACT.Silu, bias=pcol("ln_b", c), scale=pcol("ln_g", c))
                            last.then_inc(silu_done, 1)
                    with act.Fori(0, KC) as m:
                        act.wait_ge(gates_free, m + 1)
                        for s in range(RING):
                            step("MIXG", m, s, gates[:, s, :], ACT.Sigmoid, following=WIDTH["MIXP"],
                                 bias=par[:, bass.ds(m * 4 + (PCOL["b_gate"] + s), 1)])
                        for s in range(RING):
                            ahead("MIXP", m, s)
                    act.wait_ge(y_ready, 2)
                    for m in "dbca":
                        act.dma_start(ext_out[m][layer], ext[m][:, :, TP:TP + tail(m)]).then_inc(stored, 16)
                    act.dma_start(h_out[layer], h_last[:, :, :]).then_inc(stored, 16)
                    with act.Fori(0, 2) as g:
                        for s in range(RING):
                            step("OUT", g, s, mixed[:, 4 * g + s, :])
                    act.wait_ge(added, 1)
                    norm_square(act)
                    act.dma_start(x_keep.rearrange("p (k t) -> p k t", k=KC), x[:, :, :]).then_inc(x_saved, 16)
                    root(act, 2)
                    norm_high(act, 1)
                    act.wait_ge(stored, 16 * 5)
                    with act.Fori(0, 3) as g:
                        for s in range(RING):
                            step("WQ", g, s, q_high[:, 4 * g + s, 0:T], signal=q_high_out)
                    for s in range(RING):
                        step("WQ", 3, s, q_high[:, 12 + s, 0:T], signal=q_high_out, following=WIDTH["KEYS"])
                    for s in range(RING):
                        ahead("KEYS", 0, s)
                    with act.Fori(0, UTAIL) as g:
                        for s in range(RING):
                            step("U", g, s, acts[:, 4 * g + s, :], ACT.Gelu_apprx_tanh)
                    act.wait_ge(selected, TILES)
                    A(routed[:, :, 2, :], routed[:, :, 2, :], ACT.Exp).then_inc(weighed, 1)
                    act.wait_ge(x_saved, 16)
                    with act.Fori(UTAIL, GROUPS["U"]) as g:
                        for s in range(RING):
                            step("U", g, s, acts[:, 4 * g + s, :], ACT.Gelu_apprx_tanh)
                    act.wait_ge(spread_out, T // 4 + 2)

                    def c_split(i, s):
                        A(c_high[:, s % 2, :], acts[:, i, :], ACT.Copy).then_inc(c_high_out, 1)

                    c_split(0, 0)
                    c_split(1, 1)
                    with act.Fori(0, GROUPS["V"] - 1) as g:
                        for s in range(RING):
                            ahead("V", g, s)
                            c_split(4 * g + (s + 2), s)
                    for s in range(2):
                        ahead("V", GROUPS["V"] - 1, s)
                        c_split(NKEYS - 2 + s, s)

                @block.vector
                def _(dve):
                    V = nc.vector
                    steps = Steps(dve, v_step)
                    did, settle = steps.did, steps.settle

                    def conv(m, out, bias):
                        e, taps, n = ext[m], CONV[m], CHUNKS[m]
                        col = PCOL["conv_" + m]

                        def tap(j):
                            for c in range(n):
                                w = par[:, bass.ds(j * n + (col + c), 1)]
                                pr = e[:, c, bass.ds(j, TP)]
                                w4 = e[:, c, PAD[m] + TP:row(m)].rearrange("p (b w) -> p b w", b=NB)
                                sa = w4[:, :, bass.ds(j, TS)]
                                o_p, o_s = out[:, c, 0:TP], by_seq(out[:, c, :])
                                if isinstance(j, int):
                                    b = pcol(bias, c) if bias else 0.0
                                    did(V.tensor_scalar(o_p, pr, w, b, ALU.mult, ALU.add))
                                    did(V.tensor_scalar(o_s, sa, w, b, ALU.mult, ALU.add))
                                else:
                                    did(V.scalar_tensor_tensor(o_p, pr, w, o_p, ALU.mult, ALU.add))
                                    did(V.scalar_tensor_tensor(o_s, sa, w, o_s, ALU.mult, ALU.add))

                        tap(0)

                        def body(j):
                            settle()
                            tap(j + 1)
                        steps.loop(taps - 1, body, 2 * n)
                        settle()

                    def split(src, name, signal=None):
                        high, low = pair[name]
                        did(V.tensor_copy(high, src))
                        settle()
                        last = V.tensor_tensor(low, src, high.bitcast(F32), ALU.subtract)
                        if signal is None:
                            did(last)
                        else:
                            last.then_inc(signal, 1)

                    V.sem_inc(gates_free, 1)
                    dve.wait_ge(par_in, 16)
                    norm_scale(dve, steps, 0, 1, par[:, PCOL["norm1"]:PCOL["norm1"] + KC])
                    norm_low(dve, 0)
                    did(V.tensor_scalar(lru[:, 0, :], pcol("lam", 0, CC), -1.0, None, ALU.mult))
                    settle()
                    V.tensor_tensor(lru[:, 0, :], lru[:, 0, :], pcol("lam", 0, CC), ALU.max).then_inc(softplus_arg, 1)
                    dve.wait_ge(softplus_exp, 1)
                    did(V.tensor_scalar(lru[:, 2, :], lru[:, 1, :], 2.0, None, ALU.add))
                    settle()
                    did(V.reciprocal(lru[:, 2, :], lru[:, 2, :]))
                    settle()
                    did(V.tensor_tensor(lru[:, 3, :], lru[:, 1, :], lru[:, 2, :], ALU.mult))
                    settle()
                    did(V.tensor_tensor(lru[:, 4, :], lru[:, 3, :], lru[:, 3, :], ALU.mult))
                    settle()
                    did(V.tensor_scalar(lru[:, 5, :], lru[:, 4, :], 2.0 / 17, 2.0 / 15, ALU.mult, ALU.add))
                    for k in (13, 11, 9, 7, 5, 3, 1):
                        settle()
                        did(V.tensor_tensor(lru[:, 5, :], lru[:, 5, :], lru[:, 4, :], ALU.mult))
                        settle()
                        did(V.tensor_scalar(lru[:, 5, :], lru[:, 5, :], 2.0 / k, None, ALU.add))
                    settle()
                    did(V.tensor_tensor(lru[:, 5, :], lru[:, 5, :], lru[:, 3, :], ALU.mult))
                    did(V.tensor_scalar(lru[:, 2, :], pcol("lam", 0, CC), -1.0, 0.0, ALU.mult, ALU.max))
                    settle()
                    did(V.tensor_tensor(lru[:, 5, :], lru[:, 5, :], lru[:, 2, :], ALU.add))
                    settle()
                    V.tensor_scalar(lru[:, 6, :], lru[:, 5, :], -LRU_C, None, ALU.mult)
                    V.tensor_scalar(lru[:, 7, :], lru[:, 5, :], LRU_C, None, ALU.mult).then_inc(softplus_done, 1)

                    dve.wait_ge(padded, 1)
                    dve.wait_ge(ext_loaded, 16 * 5)
                    dve.wait_ge(evacuated, EVAC["D"] + 8)
                    did(V.tensor_tensor(prompt_of(ext["d"], "d"), d_val[:, :, 0:TP], d_gate[:, :, 0:TP], ALU.mult))
                    did(V.tensor_tensor(samples_of(ext["d"], "d"), by_seq_all(d_val), by_seq_all(d_gate), ALU.mult))
                    settle()
                    conv("d", cd, "conv_d_b")
                    V.sem_inc(d_conv, 1)

                    dve.wait_ge(evacuated, EVAC["B"] + 4)
                    for c in range(CA):
                        src, dst, valid = ext["b"][:, c, :], wins[0], 0
                        for level in range(c + 1):
                            d = 1 << level
                            valid += d
                            did(V.tensor_tensor(dst[:, valid:row("b")], src[:, valid:row("b")],
                                                src[:, valid - d:row("b") - d], ALU.add))
                            settle()
                            src, dst = dst, wins[1] if dst is wins[0] else wins[0]
                        w = 2 << c
                        a = PAD["b"]
                        win = src[:, a + TP:row("b")].rearrange("p (b w) -> p b w", b=NB)[:, :, a:a + TS]
                        did(V.scalar_tensor_tensor(p_b[:, c, 16:TP], src[:, a + 16:a + TP], 1.0 / w,
                                                   ext["b"][:, c, a + 16:a + TP], ALU.mult, ALU.subtract))
                        did(V.scalar_tensor_tensor(by_seq(p_b[:, c, :]), win, 1.0 / w, samples_of(ext["b"], "b", c),
                                                   ALU.mult, ALU.subtract))
                        did(V.tensor_tensor(p_b[:, c, 0:16], src[:, a:a + 16], first_cnt[:, c, :], ALU.mult))
                        settle()
                        did(V.tensor_tensor(p_b[:, c, 0:16], p_b[:, c, 0:16], ext["b"][:, c, a:a + 16], ALU.subtract))
                    settle()
                    split(p_b, "p_b", pooled)

                    dve.wait_ge(ln_sum1, 1)
                    did(V.tensor_scalar(stat[:, 0, :], bank[4][:, 0:T], 1.0 / W_D, None, ALU.mult))
                    settle()
                    V.tensor_tensor(cd, cd, stat[:, 0:1, :].to_broadcast([P, CA, T]), ALU.subtract).then_inc(ln_centred, 1)

                    dve.wait_ge(evacuated, EVAC["C"] + 8)
                    conv("c", xconv, "conv_c_b")
                    split(xconv, "xconv", c_conv)
                    dve.wait_ge(extra_out, 4)
                    split(y_b, "b")

                    dve.wait_ge(lru_exp, 1)
                    did(V.tensor_tensor(ig, ig, xconv, ALU.mult))
                    settle()
                    did(V.tensor_scalar(xconv, rg, 0.5, 0.5, ALU.mult, ALU.add))
                    settle()
                    did(V.reciprocal(xconv, xconv))
                    settle()
                    V.tensor_tensor(rg, rg, xconv, ALU.mult).then_inc(lru_ratio, 1)
                    dve.wait_ge(ln_sum2, 1)
                    did(V.tensor_scalar(stat[:, 0, :], bank[4][:, 0:T], 1.0 / W_D, EPS, ALU.mult, ALU.add))
                    settle()
                    V.reciprocal(stat[:, 0, :], stat[:, 0, :]).then_inc(inverse, 1)
                    dve.wait_ge(lru_root, 1)
                    did(V.tensor_tensor(ig, ig, rg, ALU.mult))
                    did(V.tensor_tensor(h0a[:, :, :], by_seq_all(aa)[:, :, :, 0], h0[:, :, :], ALU.mult))
                    settle()
                    did(V.tensor_tensor(by_seq_all(ig)[:, :, :, 0], by_seq_all(ig)[:, :, :, 0], h0a[:, :, :], ALU.add))
                    did(V.memset(by_seq_all(aa)[:, :, :, 0], 0.0))
                    did(V.memset(aa[:, :, 0:1], 0.0))
                    settle()
                    flat = [v.rearrange("p c t -> p (c t)") for v in (xconv, aa, ig)]
                    did(V.tensor_tensor_scan(flat[0], flat[1], flat[2], 0.0, ALU.mult, ALU.add))
                    dve.wait_ge(rooted, 2)
                    V.tensor_tensor(cd, cd, stat[:, 1:2, :].to_broadcast([P, CA, T]), ALU.mult).then_inc(ln_scaled, 1)
                    settle()
                    did(V.tensor_copy(h_last[:, :, 0:1], xconv[:, :, TP - 1:TP]))
                    did(V.tensor_copy(h_last[:, :, 1:1 + NB], by_seq_all(xconv)[:, :, :, TS - 1]))
                    V.tensor_tensor(rg, xconv, yg, ALU.mult).then_inc(y_ready, 1)
                    dve.wait_ge(y_ready, 1)
                    split(rg, "c")
                    dve.wait_ge(silu_done, 1)
                    split(cd, "d")

                    dve.wait_ge(evacuated, EVAC["A"] + 12)
                    gb, gc, xv = ua[:, 0:CA, :], ua[:, CA:2 * CA, :], ua[:, 2 * CA:3 * CA, :]
                    did(V.tensor_tensor(prompt_of(ext["a"], "a"), gc[:, :, 0:TP], xv[:, :, 0:TP], ALU.mult))
                    did(V.tensor_tensor(samples_of(ext["a"], "a"), by_seq_all(gc), by_seq_all(xv), ALU.mult))
                    settle()
                    conv("a", y_a, None)
                    V.tensor_tensor(y_a, y_a, gb, ALU.mult).then_inc(y_ready, 1)
                    dve.wait_ge(y_ready, 2)
                    split(y_a, "a", chunk_merged)
                    dve.wait_ge(chunk_merged, 1)

                    m_high, m_low = pair["merged"]

                    def mix(m):
                        dve.wait_ge(half_done, 2 * number("MIXP", m, 3) + 2)
                        dve.wait_ge(evacuated, EVAC["MIXG"] + 4 * m + 4)
                        for b in range(4):
                            ins = V.tensor_tensor(prod[:, b, :], bank[4 + b][:, 0:T], gates[:, b, :], ALU.mult)
                            if b < 3:
                                did(ins)
                        ins.then_inc(gates_free, 1)
                        dve.wait_ge(gates_free, m + 2)
                        did(V.tensor_tensor(prod[:, 0:2, :], prod[:, 0:2, :], prod[:, 2:4, :], ALU.add))
                        settle()
                        did(V.tensor_tensor(prod[:, 0, :], prod[:, 0, :], prod[:, 1, :], ALU.add))
                        settle()
                        did(V.tensor_copy(m_high[:, m, :], prod[:, 0, :]))
                        settle()
                        V.tensor_tensor(m_low[:, m, :], prod[:, 0, :], m_high[:, m, :].bitcast(F32), ALU.subtract)\
                         .then_inc(chunk_merged, 1)
                        dve.wait_ge(chunk_merged, m + 2)
                    steps.loop(KC, mix, 6)

                    dve.wait_ge(evacuated, EVAC["OUT"] + 8)
                    V.tensor_tensor(x[:, :, :], x[:, :, :], mixed, ALU.add).then_inc(added, 1)
                    dve.wait_ge(added, 1)
                    norm_scale(dve, steps, 1, 3, par[:, PCOL["norm2"]:PCOL["norm2"] + KC])
                    norm_low(dve, 1)

                    dve.wait_ge(stored, 16 * 5)
                    did(V.memset(q_high[:, :, T:QCOLS].bitcast(U32), 0))
                    did(V.memset(q_low[:, :, T:QCOLS].bitcast(U32), 0))
                    settle()

                    with dve.Fori(0, 4) as g:
                        for s in range(RING):
                            dve.wait_ge(q_high_out, RING * g + (s + 1))
                            c = 4 * g + s
                            V.tensor_tensor(q_low[:, c, 0:T], bank[s][:, 0:T], q_high[:, c, 0:T].bitcast(F32),
                                            ALU.subtract).then_inc(evacuated, 1)

                    n = 0
                    for s in range(RING):
                        for tt in range(TILES):
                            if tt < TILES - 1:
                                dve.wait_ge(scores_done, 2 * s + tt + 1)
                            else:
                                dve.wait_ge(half_done, 2 * number("KEYS", 0, s) + 2)
                            V.tensor_copy(s_all[:, tt, s * 512:(s + 1) * 512], bank[4 + n % 4][:, :])\
                             .then_inc(scores_out, 1)
                            n += 1
                    dve.wait_ge(scores_out, n)

                    routing = Steps(dve, route_step)
                    did_r, settle_r = routing.did, routing.settle

                    def top16(src, values, where):
                        for r in range(4):
                            did_r(V.max(values(r)[:, 0:8], src(r)))
                        settle_r()
                        for r in range(4):
                            did_r(V.max_index(where(r)[:, 0:8], values(r)[:, 0:8], src(r)))
                        n = src(0).shape[-1]
                        for r in range(4):
                            did_r(V.match_replace(left[:, r, 0:n], values(r)[:, 0:8], src(r), NEG))
                        settle_r()
                        for r in range(4):
                            did_r(V.max(values(r)[:, 8:16], left[:, r, 0:n]))
                        settle_r()
                        for r in range(4):
                            did_r(V.max_index(where(r)[:, 8:16], values(r)[:, 8:16], left[:, r, 0:n]))
                        settle_r()

                    def route(tt):
                        did_r(V.tensor_copy(eq, s_all[:, tt, :]))
                        settle_r()
                        for q in range(HC // 4):
                            top16(lambda r: s_work[:, 4 * q + r, :], lambda r: vals[:, 4 * q + r, :],
                                  lambda r: idxs[:, 4 * q + r, :])
                        did_r(V.tensor_copy(idxf[:, :, :], idxs[:, :, :]))
                        v4 = vals[:, :, :].rearrange("p (h c) k -> p h c k", c=2)
                        first = v4[:, :, 0, :].unsqueeze(3).to_broadcast([P, HEADS, TOPK, TOPK])
                        second = v4[:, :, 1, :].unsqueeze(2).to_broadcast([P, HEADS, TOPK, TOPK])
                        did_r(V.tensor_tensor(cand.rearrange("p h (a b) -> p h a b", a=TOPK), first, second, ALU.add))
                        settle_r()
                        for q in range(HEADS // 4):
                            top16(lambda r: cand[:, 4 * q + r, :], lambda r: best[:, 4 * q + r, :],
                                  lambda r: pos[:, 4 * q + r, :])
                        pf = pos[:, :, :].rearrange("p h k -> p (h k)")
                        did_r(V.tensor_scalar(posab[:, 0, :], pf, 4, None, ALU.logical_shift_right))
                        did_r(V.tensor_scalar(posab[:, 1, :], pf, 15, None, ALU.bitwise_and))
                        settle_r()
                        did_r(V.tensor_copy(posf[:, :, :], posab[:, :, :]))
                        settle_r()
                        i4 = idxf[:, :, :].rearrange("p (h c) k -> p h c k", c=2)
                        e4 = eq.rearrange("p (h k j) -> p h k j", h=HEADS, k=TOPK)
                        e3 = eq.rearrange("p (s j) -> p s j", j=TOPK)
                        for c in range(2):
                            did_r(V.tensor_tensor(e3, posf[:, c, :].unsqueeze(2).to_broadcast([P, HK, TOPK]),
                                                iota16[:, :].unsqueeze(1).to_broadcast([P, HK, TOPK]), ALU.is_equal))
                            settle_r()
                            did_r(V.tensor_tensor(e4, e4, i4[:, :, c, :].unsqueeze(2).to_broadcast([P, HEADS, TOPK, TOPK]),
                                                ALU.mult))
                            settle_r()
                            did_r(V.tensor_reduce(routed[:, tt, c, :], e3, AX.X, ALU.add))
                            settle_r()
                        V.tensor_tensor(routed[:, tt, 2, :].rearrange("p (h k) -> p h k", h=HEADS), best[:, :, :],
                                        best[:, :, 0:1].to_broadcast([P, HEADS, TOPK]), ALU.subtract)\
                         .then_inc(selected, 1)
                        routing.restart()
                    with dve.Fori(0, TILES) as tt:
                        route(tt)
                    dve.wait_ge(weighed, 1)
                    w3 = routed[:, :, 2, :].rearrange("p t (h k) -> p t h k", h=HEADS)
                    d3 = denom[:, :].rearrange("p (t h) -> p t h", t=TILES)
                    did(V.tensor_reduce(d3, w3, AX.X, ALU.add))
                    settle()
                    did(V.reciprocal(denom[:, :], denom[:, :]))
                    settle()
                    V.tensor_tensor(w3, w3, d3.unsqueeze(3).to_broadcast([P, TILES, HEADS, TOPK]), ALU.mult)\
                     .then_inc(gated, 1)
                    dve.wait_ge(turned, 1)
                    for j in range(3):
                        last = V.tensor_copy(selT[:, j, :], bank[4 + j][:, 0:T])
                    last.then_inc(turned_out, 1)
                    dve.wait_ge(turned_out, 1)
                    dve.wait_ge(evacuated, EVAC["U"] + NKEYS)

                    def onehots_of(g, b):
                        for t in range(4):
                            c = 8 * g + (4 * b + t)
                            V.tensor_scalar(onehot[b][:, 0, t, :], iota[:, :], selT[:, 0, bass.ds(c, 1)], selT[:, 2, bass.ds(c, 1)],
                                            ALU.is_equal, ALU.mult)
                            last = V.tensor_scalar(onehot[b][:, 1, t, :], iota[:, :], selT[:, 1, bass.ds(c, 1)], None,
                                                   ALU.is_equal)
                        last.then_inc(onehots, 1)

                    def weigh(g, b):
                        a = acts[:, :, bass.ds(8 * g + 4 * b, 4)]
                        V.tensor_tensor(a, a, bank[6 + b][:, :].rearrange("p (t i) -> p i t", t=4), ALU.mult)\
                         .then_inc(spread_out, 1)

                    V.sem_inc(spread_out, 2)
                    onehots_of(0, 0)
                    onehots_of(0, 1)
                    with dve.Fori(0, T // 8 - 1) as g:
                        for b in range(2):
                            dve.wait_ge(spread, 2 * g + (b + 1))
                            weigh(g, b)
                            onehots_of(g + 1, b)
                    for b in range(2):
                        dve.wait_ge(spread, 2 * (T // 8 - 1) + b + 1)
                        weigh(T // 8 - 1, b)
                    dve.wait_ge(spread_out, T // 4 + 2)
                    with dve.Fori(0, GROUPS["V"]) as g:
                        for s in range(RING):
                            dve.wait_ge(c_high_out, RING * g + (s + 1))
                            V.tensor_tensor(c_low[:, s % 2, :], acts[:, 4 * g + s, :], c_high[:, s % 2, :].bitcast(F32),
                                            ALU.subtract).then_inc(c_low_out, 1)
                    dve.wait_ge(half_done, 2 * TOTAL)
                    dve.wait_ge(x_loaded, 16)
                    for c in range(KC):
                        did(V.tensor_tensor(x[:, c, :], x_back[:, c, :], bank[c][:, 0:T], ALU.add))
                    settle()

            nc.sync.sem_clear(range(first_sem.num, last_sem.num + 1))
            nc.all_engine_barrier()

        with nc.Block() as block:
            @block.scalar
            def _(act):
                norm_square(act)
                root(act, 0)
                act.wait_ge(x_raw, KC)
                act.dma_start(y_out.rearrange("p (k t) -> p k t", k=KC), xnf).then_inc(stored, 16)
                act.wait_ge(stored, 16)

            @block.tensor
            def _(pe):
                norm_sum(pe, 0)

            @block.vector
            def _(dve):
                norm_scale(dve, Steps(dve, v_step), 0, 1, final_g[:, :])


def kernel(**inputs):
    import numpy as np
    import concourse.bacc as bacc
    from concourse.bass_utils import run_bass_kernel_spmd

    a = {k: np.asarray(v) for k, v in inputs.items()}
    f32 = np.float32

    def columns(v, j=1):
        v = v.reshape(DEPTH, -1, P)
        return v.transpose(0, 2, 1)

    def gate_columns(v):
        return v.reshape(DEPTH, 4, KC, P).transpose(0, 3, 2, 1).reshape(DEPTH, P, 4 * KC)

    packs = {"norm1": columns(a["norm1_g"]), "norm2": columns(a["norm2_g"]), "b_gate": gate_columns(a["b_gate"]),
             "conv_a": columns(a["conv_a_w"]), "pool_scale": columns(a["pool_scale"]), "conv_c": columns(a["conv_c_w"]),
             "conv_c_b": columns(a["conv_c_b"]), "ba": columns(a["lru_ba"]), "bi": columns(a["lru_bi"]),
             "lam": columns(a["lru_lambda"]), "conv_d": columns(a["conv_d_w"]), "conv_d_b": columns(a["conv_d_b"]),
             "ln_g": columns(a["ln_d_g"]), "ln_b": columns(a["ln_d_b"])}
    params = np.concatenate([packs[n] for n, _ in PARAMS], axis=2)

    def tiles(w):
        l, d, n = w.shape
        return w.reshape(l, d // P, P, n // P, P).transpose(0, 3, 2, 1, 4).reshape(l, n // P, P, d)

    wt = tiles(a["w_in"])
    off_b, off_c, off_d, off_g = 12, 16, 32, 40
    order = [off_d + i for i in range(8)] + [off_b + i for i in range(4)] + [off_c + i for i in range(16)]
    order += list(range(12)) + [off_g + 8 * b + m for m in range(KC) for b in range(4)]
    w_in = wt[:, order]

    def ext_rows(s, m):
        v = s.reshape(DEPTH, NB, PAD[m], CHUNKS[m], P).transpose(0, 4, 3, 1, 2)
        out = np.zeros((DEPTH, P, CHUNKS[m], NB, PAD[m] + TS), f32)
        out[..., :PAD[m]] = v
        return out.reshape(DEPTH, P, CHUNKS[m], NB * (PAD[m] + TS))

    xt = np.concatenate([a["x_prompt"].reshape(TP, DM), a["x_sample"].reshape(NB * TS, DM)])
    arrays = {
        "x_in": xt.reshape(T, KC, P).transpose(2, 1, 0).reshape(P, KC * T),
        "params_in": params,
        "final_in": a["final_g"].reshape(KC, P).T,
        "pool_first": np.broadcast_to(np.array([[1.0 / min(t + 1, 2 << g) for t in range(16)] for g in range(CA)], f32),
                                      (P, CA, 16)),
        "ext_a": ext_rows(a["state_conv_a"], "a"), "ext_b": ext_rows(a["state_pool"], "b"),
        "ext_c": ext_rows(a["state_conv_c"], "c"), "ext_d": ext_rows(a["state_conv_d"], "d"),
        "h0_in": a["state_lru_h"].reshape(DEPTH, NB, CC, P).transpose(0, 3, 2, 1),
        "w_in_t": w_in,
        "w_pool": a["pool_w"].transpose(0, 2, 1, 3).reshape(DEPTH, P, CA * P),
        "w_lru": np.stack([a["lru_wa"].transpose(0, 2, 1, 3), a["lru_wi"].transpose(0, 2, 1, 3)], 1)
                   .reshape(DEPTH, 2, P, CC * P),
        "w_ab": np.stack([tiles(a["w_pa"]), tiles(a["w_pb"])], axis=1),
        "w_c": tiles(a["w_pc"]), "w_d": tiles(a["w_pd"]), "w_out_t": tiles(a["w_out"]), "w_q": tiles(a["peer_wq"]),
        "w_keys": a["peer_keys"].reshape(DEPTH, 4, 4, NKEYS, P).transpose(0, 1, 4, 2, 3).reshape(DEPTH, 4, P, 4 * P),
        "w_u": a["peer_u"].reshape(DEPTH, NKEYS, NKEYS, KC, P).transpose(0, 2, 4, 3, 1).reshape(DEPTH, NKEYS, P, DM),
        "w_v": a["peer_v"].reshape(DEPTH, NKEYS, NKEYS, DM).transpose(0, 2, 1, 3),
    }
    arrays = {k: np.ascontiguousarray(v) for k, v in arrays.items()}

    nc = bacc.Bacc("TRN2", target_bir_lowering=False, num_devices=1)

    def dram(name, shape, kind):
        return nc.dram_tensor(name, shape, F32, kind=kind).ap()

    i = {k: dram(k, v.shape, "ExternalInput") for k, v in arrays.items()}
    y = dram("y_out", (P, KC * T), "ExternalOutput")
    ext_out = {m: dram(f"ext_out_{m}", (DEPTH, P, CHUNKS[m], tail(m)), "ExternalOutput") for m in "abcd"}
    h_out = dram("h_out", (DEPTH, P, CC, 1 + NB), "ExternalOutput")
    build(nc, i["x_in"], i["params_in"], i["final_in"], i["pool_first"], {m: i[f"ext_{m}"] for m in "abcd"}, i["h0_in"],
          i["w_in_t"], i["w_pool"], i["w_lru"], i["w_ab"], i["w_c"], i["w_d"], i["w_out_t"], i["w_q"], i["w_keys"],
          i["w_u"], i["w_v"], nc.dram_tensor("x_keep", (P, KC * T), F32).ap(), y, ext_out, h_out)
    r = run_bass_kernel_spmd(nc, [arrays], core_ids=[0]).results[0]

    yt = r["y_out"].reshape(P, KC, T).transpose(2, 1, 0).reshape(T, DM)
    outs = [yt[:TP].reshape(1, TP, DM), yt[TP:].reshape(NB, TS, DM)]

    def states(m):
        e = r[f"ext_out_{m}"]
        p = e[..., :PAD[m]].transpose(0, 3, 2, 1).reshape(DEPTH, 1, PAD[m], CHUNKS[m] * P)
        s = e[..., PAD[m]:].reshape(DEPTH, P, CHUNKS[m], NB, PAD[m] + TS)[..., TS:]
        return [p, s.transpose(0, 3, 4, 2, 1).reshape(DEPTH, NB, PAD[m], CHUNKS[m] * P)]

    h = r["h_out"].transpose(0, 3, 2, 1).reshape(DEPTH, 1 + NB, DM)
    outs += states("a") + states("b") + states("c") + [h[:, :1], h[:, 1:]] + states("d")
    return tuple(np.ascontiguousarray(o) for o in outs)
```

```python
from contextlib import ExitStack

import concourse.bass as bass
from concourse import mybir

F32 = mybir.dt.float32
F32R = mybir.dt.float32r
U32 = mybir.dt.uint32
ALU = mybir.AluOpType
ACT = mybir.ActivationFunctionType
AX = mybir.AxisListType

P = 128
DM = 1024
KC = DM // P
TP, NB, TS = 256, 8, 4
T = TP + NB * TS
DEPTH = 2
EPS = 1e-6
RING = 4
W_A = W_B = W_D = DM // 2
CA = W_A // P
CC = DM // P
CONV = {"a": 3, "c": 4, "d": 31}
POOL_BUF = 15
PAD = {"a": 2, "b": POOL_BUF, "c": 3, "d": 30}
CHUNKS = {"a": CA, "b": CA, "c": CC, "d": CA}
LRU_C = 8.0
HEADS, TOPK, NKEYS = 8, 16, 128
HK = HEADS * TOPK
HC = HEADS * 2
TILES = 3
TILE_ROWS = [128, 128, 32]
NEG = -3.0e38


def row(m):
    return PAD[m] + TP + NB * (PAD[m] + TS)


def tail(m):
    return PAD[m] + NB * (PAD[m] + TS)


PARAMS = [("norm1", KC), ("norm2", KC), ("b_gate", 4 * KC), ("conv_a", 3 * CA), ("pool_scale", CA),
          ("conv_c", 4 * CC), ("conv_c_b", CC), ("ba", CC), ("bi", CC), ("lam", CC), ("conv_d", 31 * CA),
          ("conv_d_b", CA), ("ln_g", CA), ("ln_b", CA)]
PCOL = {}
_n = 0
for _name, _w in PARAMS:
    PCOL[_name] = _n
    _n += _w
NPAR = _n

SECTIONS = [("B", 1, (8, 8, 8, 8)), ("C", 4, (8, 8, 8, 8)), ("S", 1, (4, 8, 4, 4)), ("D", 2, (8, 8, 8, 8)),
            ("A", 3, (8, 8, 8, 8)), ("XB", 4, (8, 4, 8, 4)), ("XC", 4, (8, 8, 8, 8)), ("XA", 4, (8, 4, 8, 4)),
            ("DG", 2, (8, 8, 8, 8)), ("DP", 2, (4, 4, 4, 4)),
            ("OUT", 2, (8, 8, 8, 8)), ("WQ", 4, (8, 8, 8, 8)), ("KEYS", 1, (4, 4, 4, 4)),
            ("U", 32, (8, 8, 8, 8)), ("VA", 9, (8, 8, 8, 8)),
            ("VB", 20, (8, 8, 8, 8)), ("VC", 3, (8, 8, 8, 8))]
GROUPS = {name: groups for name, groups, _ in SECTIONS}
WIDTH = {name: widths for name, _, widths in SECTIONS}
FIRST, _n = {}, 0
for _name, _groups, _w in SECTIONS:
    FIRST[_name] = _n
    _n += _groups
TOTAL = RING * _n


def group(name, g):
    return g + FIRST[name]


def number(name, g, s):
    return RING * group(name, g) + s


def landed_count(name, g):
    return 16 * group(name, g) + 16


EVAC = {"B": 0, "C": 4, "D": 20, "A": 28, "XB": 40, "XC": 48, "XA": 56, "DG": 64, "OUT": 72, "WQ": 80, "U": 96}
BRANCHES = {"XB": (1, 0), "XC": (2, 1), "XA": (0, 2), "DG": (3, 3)}
UTAIL = 18
UGATED = UTAIL + 1
HALF = NKEYS // 2
BATCHES = T // 4
GGROUPS = T // 8 // RING
VA_KEYS, VA_CHUNKS, VA_PERIOD = 48, 6, 12
PERIODS = VA_KEYS * VA_CHUNKS // KC // VA_PERIOD
PERIOD_KEYS = VA_KEYS // PERIODS
QCOLS = TILES * P


class Steps:

    def __init__(self, eng, sem):
        self.eng, self.sem, self.n, self.var = eng, sem, 0, 0

    def did(self, ins):
        ins.then_inc(self.sem, 1)
        self.n += 1

    def settle(self):
        self.eng.wait_ge(self.sem, self.n + self.var)

    def restart(self):
        self.eng.wait_ge(self.sem, self.n)
        self.eng.sem_clear(self.sem)
        self.n = 0

    def loop(self, count, body, per):
        before = self.n
        with self.eng.Fori(0, count) as i:
            self.var = i * per
            body(i)
            assert self.n == before + per, (self.n - before, per)
        self.var = 0
        self.n = before + per * count


def build(nc, x_in, params_in, final_in, pool_first, ext_in, h0_in, w_in, w_pool, w_lru, w_ab, w_c, w_d, w_out,
          w_q, w_keys, w_u, w_v, x_keep, y_out, ext_out, h_out):
    with ExitStack() as ctx:
        def sem(name):
            return ctx.enter_context(nc.semaphore(name))

        words = 53200
        start = (nc.sbuf_base + 31) // 32 * 32
        ctx.enter_context(nc.sbuf_tensor("arena", [P, words], F32))

        def place(name, offset, shape, dt=F32):
            n = 1
            for d in shape:
                n *= d
            assert offset + n <= words, name
            return nc.alloc_sbuf_tensor_at(name, [P] + list(shape), dt, offset=start + 4 * offset)

        o_x = NKEYS * T
        xh = place("xn_high", o_x, [KC, T], F32R)
        xl = place("xn_low", o_x + KC * T, [KC, T], F32R)
        o_w = o_x + 2 * KC * T
        raw = [place(f"raw{s}", o_w + s * DM, [KC, P]) for s in range(RING)]
        w_high = [place(f"w_high{s}", o_w + 4 * DM + s * 512, [4, P], F32R) for s in range(RING)]
        w_low = [place(f"w_low{s}", o_w + 6 * DM + s * 512, [4, P], F32R) for s in range(RING)]
        cursor = [o_w + 8 * DM]

        def keep(name, shape, dt=F32):
            n = 1
            for d in shape:
                n *= d
            at = cursor[0]
            cursor[0] += (n + 7) // 8 * 8
            return place(name, at, shape, dt)

        par = keep("par", [NPAR])
        final_g = keep("final_g", [KC])
        first_cnt = keep("first_cnt", [CA, 16])
        ones = keep("ones", [P])
        iota = keep("iota", [P])
        ident = keep("ident", [P])
        iota16 = keep("iota16", [TOPK])
        routed = keep("routed", [TILES, 3, HK])
        denom = keep("denom", [TILES * HEADS])
        selT = keep("selT", [3, T])

        offs, at = {}, 0
        for m in "abcd":
            offs["ext_" + m] = at
            at += (CHUNKS[m] * row(m) + 7) // 8 * 8
        for name, c in (("d_val", CA), ("d_gate", CA), ("cd", CA), ("ua", 3 * CA), ("xconv", CC), ("yg", CC), ("rg", CC),
                        ("ig", CC), ("aa", CC), ("p_b", CA), ("y_a", CA), ("yb_high", CA), ("yb_low", CA), ("prod", 4)):
            offs[name] = at
            at += c * T
        o_stat = at
        o_res = NKEYS * T - KC * T
        assert o_stat + 2 * T + 200 + 8 * CC <= o_res
        ext = {m: place("ext_" + m, offs["ext_" + m], [CHUNKS[m], row(m)]) for m in "abcd"}

        def over(name, slot, c, dt=F32, skip=0):
            return place(name, offs[slot] + skip * T, [c, T], dt)[:, :, :]

        d_val, d_gate, cd = over("d_val", "d_val", CA), over("d_gate", "d_gate", CA), over("cd", "cd", CA)
        ua = over("ua", "ua", 3 * CA)
        xconv, yg, rg, ig, aa = (over(n, n, CC) for n in ("xconv", "yg", "rg", "ig", "aa"))
        p_b, y_a, prod = over("p_b", "p_b", CA), over("y_a", "y_a", CA), over("prod", "prod", 4)
        y_b = over("y_b", "p_b", CA)
        wins = [place(f"win{i}", offs["d_gate"] + i * 512, [row("b")])[:, :] for i in range(2)]
        gates = over("gates", "yg", KC)
        acc = over("acc", "rg", KC)
        sq = over("sq", "ig", KC)
        xnf = over("xnf", "aa", KC)
        mixed = over("mixed", "aa", KC)
        pair = {"p_b": (over("pb_high", "prod", CA, F32R), over("pb_low", "y_a", CA, F32R)),
                "xconv": (over("xc_high", "aa", CC, F32R), over("xc_low", "ua", CC, F32R)),
                "a": (over("ya_high", "ua", CA, F32R, CA), over("ya_low", "ua", CA, F32R, 2 * CA)),
                "b": (over("yb_high", "yb_high", CA, F32R), over("yb_low", "yb_low", CA, F32R)),
                "c": (over("yc_high", "aa", CC, F32R), over("yc_low", "ig", CC, F32R)),
                "d": (over("yd_high", "d_val", CA, F32R), over("yd_low", "d_gate", CA, F32R)),
                "merged": (over("merged_high", "xconv", KC, F32R), over("merged_low", "yg", KC, F32R)),
                "x": (xh[:, :, :], xl[:, :, :])}
        stat = place("stat", o_stat, [2, T])
        h_last = place("h_last", o_stat + 2 * T, [CC, 1 + NB])
        h0 = place("h0", o_stat + 2 * T + 72, [CC, NB])
        h0a = place("h0a", o_stat + 2 * T + 136, [CC, NB])
        lru = place("lru", o_stat + 2 * T + 200, [8, CC])
        x = place("x", o_res, [KC, T])
        x_back = place("x_back", VA_KEYS * T, [KC, T])
        q_high = place("q_hi", 0, [HC, QCOLS], F32R)
        q_low = place("q_lo", HC * QCOLS, [HC, QCOLS], F32R)
        acts = place("acts", 0, [NKEYS, T])
        o_r = UTAIL * RING * T
        s_all = place("s_all", o_r, [TILES, HC * NKEYS])
        eq = place("eq", o_r + 6144, [HK * TOPK])[:, :]
        s_work = eq.rearrange("p (c i) -> p c i", c=HC)
        cand = place("cand", o_r + 8192, [HEADS, 256])
        vals = place("vals", o_r + 10240, [HC, TOPK])
        idxs = place("idxs", o_r + 10496, [HC, TOPK], U32)
        idxf = place("idxf", o_r + 10752, [HC, TOPK])
        best = place("best", o_r + 11008, [HEADS, TOPK])
        pos = place("pos", o_r + 11136, [HEADS, TOPK], U32)
        posab = place("posab", o_r + 11264, [2, HK], U32)
        posf = place("posf", o_r + 11520, [2, HK])
        left = place("left", o_r + 11776, [4, 256])
        assert o_r + 12800 <= o_res
        o_one = (o_res, o_x)
        one1 = [[place(f"one1_{h}{b}", o_one[h] + b * 512, [4, P]) for b in range(2)] for h in range(2)]
        one2 = [[place(f"one2_{h}{b}", o_one[h] + (2 + b) * 512, [4, HALF]) for b in range(2)]
                for h in range(2)]
        c_high = place("c_hi", o_x + KC * T, [RING, T], F32R)
        c_low = place("c_lo", o_x + KC * T + RING * T, [RING, T], F32R)

        bank = [ctx.enter_context(nc.psum_tensor(f"bank{i}", [P, 512], F32)) for i in range(8)]

        setup_loaded, setup_made = sem("setup_loaded"), sem("setup_made")
        landed = [sem(f"landed{s}") for s in range(RING)]
        gates_free, lru_a = sem("gates_free"), sem("lru_a")
        high_done, low_done = sem("high_done"), sem("low_done")
        half_done = sem("half_done")
        evacuated = sem("evacuated")
        x_raw, x_high, x_saved, x_loaded = (sem(n) for n in ("x_raw", "x_high", "x_saved", "x_loaded"))
        q_high_out, c_high_out, c_low_out = (sem(n) for n in ("q_high_out", "c_high_out", "c_low_out"))
        par_in, ext_loaded, padded = sem("par_in"), sem("ext_loaded"), sem("padded")
        squared, sums, inverse, rooted, normed = (sem(n) for n in ("squared", "sums", "inverse", "rooted", "normed"))
        softplus_exp, softplus_arg, softplus_done = sem("softplus_exp"), sem("softplus_arg"), sem("softplus_done")
        d_conv, ln_sum1, ln_centred, ln_squared, ln_sum2, ln_scaled, silu_done = (
            sem(n) for n in ("d_conv", "ln_sum1", "ln_centred", "ln_squared", "ln_sum2", "ln_scaled", "silu_done"))
        pooled, extra_done, extra_out, c_conv = (sem(n) for n in ("pooled", "extra_done", "extra_out", "c_conv"))
        lru_exp, lru_ratio, lru_root, y_ready = (sem(n) for n in ("lru_exp", "lru_ratio", "lru_root", "y_ready"))
        chunk_merged, added = sem("chunk_merged"), sem("added")
        scores_done, scores_out, selected, weighed, gated = (
            sem(n) for n in ("scores_done", "scores_out", "selected", "weighed", "gated"))
        turned, turned_out, onehots, spread, spread_out, peer_done, peer_added = (
            sem(n) for n in ("turned", "turned_out", "onehots", "spread", "spread_out", "peer_done", "peer_added"))
        stored, v_step, route_step = sem("stored"), sem("v_step"), sem("route_step")
        first_sem, last_sem = landed[0], route_step

        def pcol(name, c, n=1):
            return par[:, PCOL[name] + c:PCOL[name] + c + n]

        def prompt_of(e, m, c=None):
            a = PAD[m]
            return e[:, :, a:a + TP] if c is None else e[:, c, a:a + TP]

        def samples_of(e, m, c=None, shift=0):
            w = PAD[m] + TS
            a = PAD[m] + TP
            v = (e[:, :, a:a + NB * w] if c is None else e[:, c, a:a + NB * w])
            v = v.rearrange("p c (b w) -> p c b w", b=NB) if c is None else v.rearrange("p (b w) -> p b w", b=NB)
            lo = PAD[m] - shift
            return v[:, :, :, lo:lo + TS] if c is None else v[:, :, lo:lo + TS]

        def by_seq(v):
            return v[:, TP:T].rearrange("p (b t) -> p b t", b=NB)

        def by_seq_all(v):
            return v[:, :, TP:T].rearrange("p c (b t) -> p c b t", b=NB)

        def norm_square(act):
            nc.scalar.activation(sq, x[:, :, :], ACT.Square).then_inc(squared, 1)

        def norm_sum(pe, n):
            pe.wait_ge(squared, n + 1)
            for k in range(KC):
                last = nc.tensor.matmul(bank[4][:, 0:T], ones[:, :], sq[:, k, :], start=(k == 0), stop=(k == KC - 1))
            last.then_inc(sums, 1)

        def root(act, n):
            act.wait_ge(inverse, n + 1)
            nc.scalar.activation(stat[:, 1, :], stat[:, 0, :], ACT.Sqrt).then_inc(rooted, 1)

        def norm_scale(dve, steps, n, roots, gain):
            dve.wait_ge(sums, n + 1)
            steps.did(nc.vector.tensor_scalar(stat[:, 0, :], bank[4][:, 0:T], 1.0 / DM, EPS, ALU.mult, ALU.add))
            steps.settle()
            nc.vector.reciprocal(stat[:, 0, :], stat[:, 0, :]).then_inc(inverse, 1)
            dve.wait_ge(rooted, roots)
            for k in range(KC):
                nc.vector.scalar_tensor_tensor(xnf[:, k, :], x[:, k, :], gain[:, k:k + 1], stat[:, 1, :],
                                               ALU.mult, ALU.mult).then_inc(x_raw, 1)

        def norm_high(act, n):
            for k in range(KC):
                act.wait_ge(x_raw, KC * n + k + 1)
                nc.scalar.activation(xh[:, k, :], xnf[:, k, :], ACT.Copy).then_inc(x_high, 1)

        def norm_low(dve, n):
            for k in range(KC):
                dve.wait_ge(x_high, KC * n + k + 1)
                nc.vector.tensor_tensor(xl[:, k, :], xnf[:, k, :], xh[:, k, :].bitcast(F32), ALU.subtract)\
                  .then_inc(normed, 1)

        with nc.Block() as block:
            @block.sync
            def _(sp):
                sp.dma_start(x[:, :, :], x_in.rearrange("p (k t) -> p k t", k=KC)).then_inc(setup_loaded, 16)
                sp.dma_start(final_g[:, :], final_in).then_inc(setup_loaded, 16)
                sp.dma_start(first_cnt[:, :, :], pool_first).then_inc(setup_loaded, 16)
                sp.wait_ge(setup_loaded, 48)

            @block.gpsimd
            def _(pool):
                nc.gpsimd.memset(ones[:, :], 1.0)
                nc.gpsimd.iota(iota[:, :], [[1, P]], base=0, channel_multiplier=0, allow_small_or_imprecise_dtypes=True)
                nc.gpsimd.iota(iota16[:, :], [[1, TOPK]], base=0, channel_multiplier=0,
                               allow_small_or_imprecise_dtypes=True)
                nc.gpsimd.memset(ident[:, :], 0.0).then_inc(setup_made, 1)
                pool.wait_ge(setup_made, 1)
                nc.gpsimd.affine_select(out=ident[:, :], in_=ident[:, :], compare_op=ALU.not_equal, fill=1.0, base=0,
                                        pattern=[[-1, P]], channel_multiplier=1).then_inc(setup_made, 1)
                pool.wait_ge(setup_made, 2)

        with nc.Fori(0, DEPTH) as layer:
            with nc.Block() as block:

                @block.sync
                def _(sp):
                    def load(name, g, s, src, free=True):
                        if free:
                            sp.wait_ge(low_done, 2 * number(name, g, s) - 2 * RING + 2)
                        width = WIDTH[name][s]
                        sp.dma_start(raw[s][:, 0:width, :], src.rearrange("p (k m) -> p k m", k=width))\
                          .then_inc(landed[s], 16)

                    for s in range(RING):
                        load("B", 0, s, w_in[layer, s], free=False)
                    with sp.Fori(0, 4) as g:
                        for s in range(RING):
                            load("C", g, s, w_in[layer, 4 * g + (4 + s)])
                    load("S", 0, 0, w_pool[layer])
                    load("S", 0, 1, w_lru[layer, 0])
                    for half in range(2):
                        load("S", 0, 2 + half, w_lru[layer, 1, :, 512 * half:512 * half + 512])
                    with sp.Fori(0, 5) as g:
                        for s in range(RING):
                            load("D", g, s, w_in[layer, 4 * g + (20 + s)])
                    for name, w in (("XB", w_ab[layer, 1]), ("XC", w_c[layer]), ("XA", w_ab[layer, 0])):
                        with sp.Fori(0, 4) as g:
                            for s in range(0, RING, 2):
                                load(name, g, s, w_in[layer, 2 * g + (40 + KC * BRANCHES[name][0] + s // 2)])
                                load(name, g, s + 1, w[2 * g + s // 2])
                    with sp.Fori(0, 2) as g:
                        for s in range(RING):
                            load("DG", g, s, w_in[layer, 4 * g + (40 + KC * BRANCHES["DG"][0] + s)])
                    with sp.Fori(0, 2) as g:
                        for s in range(RING):
                            load("DP", g, s, w_d[layer, 4 * g + s])
                    with sp.Fori(0, 2) as g:
                        for s in range(RING):
                            load("OUT", g, s, w_out[layer, 4 * g + s])
                    with sp.Fori(0, 4) as g:
                        for s in range(RING):
                            load("WQ", g, s, w_q[layer, 4 * g + s])
                    for s in range(RING):
                        load("KEYS", 0, s, w_keys[layer, s])
                    with sp.Fori(0, GROUPS["U"]) as g:
                        for s in range(RING):
                            load("U", g, s, w_u[layer, 4 * g + s])
                    with sp.Fori(0, 12) as g:
                        for s in range(RING):
                            load("VA", g, s, w_v[layer, 4 * g + s])
                    sp.wait_ge(x_saved, 16)
                    sp.wait_ge(half_done, 2 * number("VB", 2, 0))
                    sp.dma_start(x_back[:, :, :], x_keep.rearrange("p (k t) -> p k t", k=KC)).then_inc(x_loaded, 16)
                    with sp.Fori(12, 32) as g:
                        for s in range(RING):
                            load("VA", g, s, w_v[layer, 4 * g + s])

                @block.gpsimd
                def _(pool):
                    for m in "abcd":
                        last = nc.gpsimd.memset(ext[m][:, :, 0:PAD[m]], 0.0)
                    last.then_inc(padded, 1)

                    def low(grp, s, width=8):
                        for half in range(width // 4):
                            n = 2 if width == 4 else 1
                            pool.wait_ge(high_done, 8 * grp + (2 * s + half + n))
                            slot = 2 * (s % 2) + half
                            nc.gpsimd.tensor_tensor(w_low[slot][:, :, :], raw[s][:, 4 * half:4 * half + 4, :],
                                                    w_high[slot][:, :, :].bitcast(F32), ALU.subtract)\
                              .then_inc(low_done, n)

                    def full_groups(first, count):
                        with pool.Fori(0, count) as g:
                            for s in range(RING):
                                low(g + first, s)

                    def narrow_group(name, g):
                        for s in range(RING):
                            low(group(name, g), s, WIDTH[name][s])

                    full_groups(0, 5)
                    narrow_group("S", 0)
                    full_groups(FIRST["D"], 5)
                    for name in ("XB", "XC", "XA", "DG", "DP"):
                        with pool.Fori(0, GROUPS[name]) as g:
                            narrow_group(name, g)
                    full_groups(FIRST["OUT"], 6)
                    narrow_group("KEYS", 0)
                    full_groups(FIRST["U"], 64)

                @block.tensor
                def _(pe):
                    res = [bank[s][:, 0:T] for s in range(8)]

                    def product(out, high, low, moving, start, stop):
                        m_high, m_low = moving
                        nc.tensor.matmul(out, high, m_high, start=start, stop=False)
                        nc.tensor.matmul(out, high, m_low, start=False, stop=False)
                        return nc.tensor.matmul(out, low, m_high, start=False, stop=stop)

                    def halves(name, g, s):
                        width = WIDTH[name][s]
                        for half in range(width // 4):
                            n = 2 if width == 4 else 1
                            pe.wait_ge(low_done, 2 * number(name, g, s) + (half + n))
                            slot = 2 * (s % 2) + half
                            yield 4 * half, w_high[slot], w_low[slot], n

                    def tile(name, g, s, out, src, evac=True, first=None):
                        if evac and name != "B":
                            pe.wait_ge(evacuated, RING * g + (EVAC[name] + s - RING + 1))
                        width = WIDTH[name][s]
                        high, low = pair[src]
                        for k0, wh, wl, n in halves(name, g, s):
                            for k in range(4):
                                if first is not None:
                                    pe.wait_ge(first[0], first[1] + k0 + k + 1)
                                last = product(out, wh[:, k, :], wl[:, k, :], (high[:, k0 + k, :], low[:, k0 + k, :]),
                                               k0 + k == 0, k0 + k == width - 1)
                            last.then_inc(half_done, n)

                    norm_sum(pe, 0)
                    for s in range(RING):
                        tile("B", 0, s, res[s], "x", first=(normed, 0))
                    with pe.Fori(0, 4) as g:
                        for s in range(RING):
                            tile("C", g, s, res[s], "x")
                    n = 0
                    for s, src in enumerate(("p_b", "xconv", "xconv", "xconv")):
                        pe.wait_ge(pooled if s == 0 else c_conv, 1)
                        high, low = pair[src]
                        for k0, wh, wl, count in halves("S", 0, s):
                            k0 += 4 * (s == 3)
                            for k in range(4):
                                if n >= 4:
                                    pe.wait_ge(extra_out, n - 3)
                                last = product(res[4 + n % 4], wh[:, k, :], wl[:, k, :],
                                               (high[:, k0 + k, :], low[:, k0 + k, :]), True, True)
                                n += 1
                                last.then_inc(*((extra_done, 1) if k < 3 else (half_done, count)))
                    with pe.Fori(0, 2) as g:
                        for s in range(RING):
                            tile("D", g, s, res[s], "x")
                    with pe.Fori(0, 3) as g:
                        for s in range(RING):
                            tile("A", g, s, res[s], "x")

                    def branch(name, src):
                        turn = BRANCHES[name][1]
                        pe.wait_ge(y_ready, turn + 1)
                        with pe.Fori(0, GROUPS[name]) as g:
                            for s in range(0, RING, 2):
                                pe.wait_ge(evacuated, 2 * g + (EVAC[name] + s // 2 - 1))
                                tile(name, g, s, res[s], "x", evac=False)
                                pe.wait_ge(gates_free, 2 * g + (KC * turn + s // 2 + 1))
                                tile(name, g, s + 1, res[5 + s], src, evac=False)

                    pe.wait_ge(extra_out, 20)
                    branch("XB", "b")
                    branch("XC", "c")
                    branch("XA", "a")
                    pe.wait_ge(evacuated, EVAC["DG"])
                    for s in range(RING):
                        tile("DG", 0, s, res[s], "x", evac=False)
                    pe.wait_ge(d_conv, 1)
                    for k in range(CA):
                        last = nc.tensor.matmul(res[4], ones[:, :], cd[:, k, :], start=(k == 0), stop=(k == CA - 1))
                    last.then_inc(ln_sum1, 1)
                    for s in range(RING):
                        tile("DG", 1, s, res[s], "x")
                    pe.wait_ge(ln_squared, 1)
                    for k in range(CA):
                        last = nc.tensor.matmul(res[4], ones[:, :], d_gate[:, k, :], start=(k == 0), stop=(k == CA - 1))
                    last.then_inc(ln_sum2, 1)
                    pe.wait_ge(y_ready, 4)
                    with pe.Fori(0, 2) as g:
                        for s in range(RING):
                            pe.wait_ge(gates_free, 4 * g + (3 * KC - 1 + s))
                            tile("DP", g, s, res[4 + s], "d", evac=False)
                    for s in range(RING):
                        tile("OUT", 0, s, res[s], "merged", first=(chunk_merged, 0))
                    for s in range(RING):
                        tile("OUT", 1, s, res[s], "merged")
                    norm_sum(pe, 1)
                    for s in range(RING):
                        tile("WQ", 0, s, res[s], "x", first=(normed, KC))
                    with pe.Fori(1, 4) as g:
                        for s in range(RING):
                            tile("WQ", g, s, res[s], "x")
                    pe.wait_ge(evacuated, EVAC["WQ"] + HC)
                    n = 0
                    for s in range(RING):
                        for _, wh, wl, count in halves("KEYS", 0, s):
                            for tt in range(TILES):
                                if n >= 4:
                                    pe.wait_ge(scores_out, n - 3)
                                for c in range(4):
                                    out = bank[4 + n % 4][:, c * P:(c + 1) * P]
                                    qh = q_high[:, 4 * s + c, tt * P:(tt + 1) * P]
                                    ql = q_low[:, 4 * s + c, tt * P:(tt + 1) * P]
                                    last = product(out, qh, ql, (wh[:, c, :], wl[:, c, :]), True, True)
                                n += 1
                                last.then_inc(*((scores_done, 1) if tt < TILES - 1 else (half_done, count)))
                    def u_group(g):
                        for s in range(RING):
                            tile("U", g, s, res[s], "x")

                    with pe.Fori(0, UGATED) as g:
                        u_group(g)
                    pe.wait_ge(gated, 1)
                    for j in range(3):
                        for tt in range(TILES):
                            r = TILE_ROWS[tt]
                            last = nc.tensor.transpose(bank[4 + j][:, tt * P:tt * P + r], routed[0:r, tt, j, :],
                                                       ident[0:r, 0:r])
                    last.then_inc(turned, 1)

                    def gates_of(stage, pair_number):
                        for b in range(2):
                            n = 2 * pair_number + (BATCHES * stage + b + 1)
                            pe.wait_ge(onehots, n)
                            pe.wait_ge(spread_out, n)
                            for t in range(4):
                                last = nc.tensor.matmul(bank[6 + b][:, t * HALF:(t + 1) * HALF], one1[stage][b][:, t, :],
                                                        one2[stage][b][:, t, :], start=True, stop=True)
                            last.then_inc(spread, 1)

                    pe.wait_ge(turned_out, 1)
                    with pe.Fori(0, GGROUPS) as g:
                        for s in range(RING):
                            tile("U", g + UGATED, s, res[s], "x")
                            gates_of(0, RING * g + s)
                    with pe.Fori(UGATED + GGROUPS, GROUPS["U"]) as g:
                        u_group(g)
                    def block_product(c, slot, wh, wl, start=False, stop=False):
                        return product(res[c], wh, wl, (c_high[:, slot, :], c_low[:, slot, :]), start, stop)

                    def va_period(n, first=False):
                        for j in range(VA_PERIOD):
                            for c0, wh, wl, signal in halves("VA", 3 * n + j // RING, j % RING):
                                for c in range(4):
                                    i, chunk = divmod(KC * j + c0 + c, VA_CHUNKS)
                                    if chunk == 0:
                                        pe.wait_ge(c_low_out, PERIOD_KEYS * n + (i + 1))
                                    last = block_product(chunk, i % RING, wh[:, c, :], wl[:, c, :], start=(first and i == 0))
                                last.then_inc(half_done, signal)
                            gates_of(1, VA_PERIOD * n + j)

                    def vb_group(g, first=False, end=False):
                        for s in range(RING):
                            pe.wait_ge(c_low_out, RING * g + (VA_KEYS + s + 1))
                            for c0, wh, wl, signal in halves("VB", g, s):
                                for c in range(c0, c0 + 4):
                                    last = block_product(c, s, wh[:, c - c0, :], wl[:, c - c0, :],
                                                         start=(first and s == 0 and c >= VA_CHUNKS),
                                                         stop=(end and s == RING - 1 and c < VA_CHUNKS))
                                last.then_inc(half_done, signal)

                    def vc_group(g, end=False):
                        for s in range(RING):
                            for c0, wh, wl, signal in halves("VC", g, s):
                                for c in range(4):
                                    slot, odd = divmod(c0 + c, 2)
                                    if odd == 0:
                                        pe.wait_ge(c_low_out, 4 * RING * g + (NKEYS + 4 * s + slot + 1))
                                    last = block_product(VA_CHUNKS + odd, slot, wh[:, c, :], wl[:, c, :],
                                                         stop=(end and s == RING - 1 and slot == 3))
                                last.then_inc(half_done, signal)

                    pe.wait_ge(evacuated, EVAC["U"] + NKEYS)
                    va_period(0, first=True)
                    with pe.Fori(1, PERIODS) as n:
                        va_period(n)
                    pe.wait_ge(spread_out, 2 * BATCHES + 2)
                    vb_group(0, first=True)
                    with pe.Fori(1, GROUPS["VB"] - 1) as g:
                        vb_group(g)
                    vb_group(GROUPS["VB"] - 1, end=True)
                    with pe.Fori(0, GROUPS["VC"] - 1) as g:
                        vc_group(g)
                    vc_group(GROUPS["VC"] - 1, end=True)

                @block.scalar
                def _(act):
                    A = nc.scalar.activation

                    def split(grp, s, width=8):
                        act.wait_ge(landed[s], 16 * grp + 16)
                        for half in range(width // 4):
                            if not (isinstance(grp, int) and RING * grp + s < 2):
                                act.wait_ge(half_done, 8 * grp + (2 * s + half - 3))
                            A(w_high[2 * (s % 2) + half][:, :, :], raw[s][:, 4 * half:4 * half + 4, :], ACT.Copy)\
                                .then_inc(high_done, 2 if width == 4 else 1)

                    def ahead(name, g, s, following=(8, 8)):
                        if s < 2:
                            split(group(name, g), s + 2, WIDTH[name][s + 2])
                        else:
                            split(group(name, g) + 1, s - 2, following[s - 2])

                    def step(name, g, s, out, func=ACT.Copy, following=(8, 8), signal=evacuated, **kw):
                        ahead(name, g, s, following)
                        act.wait_ge(half_done, 2 * number(name, g, s) + 2)
                        A(out, bank[s][:, 0:T], func, **kw).then_inc(signal, 1)

                    norm_square(act)
                    act.dma_start(par[:, :], params_in[layer]).then_inc(par_in, 16)
                    for m in "bcda":
                        w = NB * (PAD[m] + TS)
                        act.dma_start(ext[m][:, :, PAD[m] + TP:PAD[m] + TP + w], ext_in[m][layer])\
                           .then_inc(ext_loaded, 16)
                    act.dma_start(h0[:, :, :], h0_in[layer]).then_inc(ext_loaded, 16)
                    split(0, 0)
                    split(0, 1)
                    root(act, 0)
                    norm_high(act, 0)
                    act.wait_ge(ext_loaded, 16 * 5)

                    def into_ext(m, name, g, s, c):
                        ahead(name, g, s)
                        act.wait_ge(half_done, 2 * number(name, g, s) + 2)
                        A(prompt_of(ext[m], m, c), bank[s][:, 0:TP], ACT.Copy)
                        A(samples_of(ext[m], m, c), by_seq(bank[s][:, 0:T]), ACT.Copy).then_inc(evacuated, 1)

                    for s in range(RING):
                        into_ext("b", "B", 0, s, s)
                    for g in range(2):
                        for s in range(RING):
                            into_ext("c", "C", g, s, 4 * g + s)
                        if g == 0:
                            act.wait_ge(softplus_arg, 1)
                            A(lru[:, 1, :], lru[:, 0, :], ACT.Exp, scale=-1.0).then_inc(softplus_exp, 1)
                    for g in range(2):
                        for s in range(RING):
                            step("C", 2 + g, s, yg[:, 4 * g + s, :], ACT.Gelu_apprx_tanh,
                                 following=(8, 8) if g == 0 else WIDTH["S"][:2])
                    n = 0
                    for s in range(RING):
                        for half in range(WIDTH["S"][s] // 4):
                            for k in range(4):
                                if k < 3:
                                    act.wait_ge(extra_done, n - n // 4 + 1)
                                else:
                                    act.wait_ge(half_done, 2 * number("S", 0, s) + (half + 1 if WIDTH["S"][s] == 8 else 2))
                                src = bank[4 + n % 4][:, 0:T]
                                c = 4 * half + k + 4 * (s == 3)
                                if s == 0:
                                    ins = A(y_b[:, c, :], src, ACT.Identity, scale=pcol("pool_scale", c))
                                elif s == 1:
                                    ins = A(rg[:, c, :], src, ACT.Sigmoid, bias=pcol("ba", c))
                                else:
                                    ins = A(ig[:, c, :], src, ACT.Sigmoid, bias=pcol("bi", c))
                                ins.then_inc(extra_out, 1)
                                n += 1
                        ahead("S", 0, s)
                    act.wait_ge(softplus_done, 1)
                    act.wait_ge(extra_out, 20)
                    for c in range(CC):
                        A(aa[:, c, :], rg[:, c, :], ACT.Exp, scale=lru[:, 6, c:c + 1]).then_inc(lru_a, 1)
                    act.wait_ge(lru_a, CC)
                    for c in range(CC):
                        last = A(rg[:, c, :], rg[:, c, :], ACT.Tanh, scale=lru[:, 7, c:c + 1])
                    last.then_inc(lru_exp, 1)
                    for s in range(RING):
                        step("D", 0, s, d_val[:, s, :])
                    for s in range(RING):
                        step("D", 1, s, d_gate[:, s, :], ACT.Sigmoid)
                    act.wait_ge(lru_ratio, 1)
                    A(rg, rg, ACT.Sqrt).then_inc(lru_root, 1)
                    for g in range(3):
                        for s in range(RING):
                            step("A", g, s, ua[:, 4 * g + s, :], following=WIDTH["XB"][:2] if g == 2 else (8, 8))

                    def gate_of(name, g, s, c, following=(8, 8)):
                        number_of, turn = BRANCHES[name]
                        if turn > 0:
                            act.wait_ge(gates_free, c + (KC * (turn - 1) + 3))
                        step(name, g, s, gates[:, c, :], ACT.Sigmoid, following=following,
                             bias=par[:, bass.ds(c + (PCOL["b_gate"] + KC * number_of), 1)])

                    def branch_group(name, g, following=None):
                        following = following or WIDTH[name][:2]
                        for s in range(0, RING, 2):
                            gate_of(name, g, s, 2 * g + s // 2, following)
                            ahead(name, g, s + 1, following)

                    act.wait_ge(y_ready, 2)
                    for name, after in (("XB", "XC"), ("XC", "XA"), ("XA", "DG")):
                        with act.Fori(0, GROUPS[name] - 1) as g:
                            branch_group(name, g)
                        branch_group(name, GROUPS[name] - 1, WIDTH[after][:2])
                    act.wait_ge(y_ready, 3)
                    for m in "bcda":
                        act.dma_start(ext_out[m][layer], ext[m][:, :, TP:TP + tail(m)]).then_inc(stored, 16)
                    act.dma_start(h_out[layer], h_last[:, :, :]).then_inc(stored, 16)
                    for s in range(RING):
                        gate_of("DG", 0, s, s)
                    act.wait_ge(ln_centred, 1)
                    A(d_gate, cd, ACT.Square).then_inc(ln_squared, 1)
                    for s in range(RING):
                        gate_of("DG", 1, s, 4 + s, WIDTH["DP"][:2])
                    root(act, 1)
                    act.wait_ge(ln_scaled, 1)
                    for c in range(CA):
                        last = A(cd[:, c, :], cd[:, c, :], ACT.Silu, bias=pcol("ln_b", c), scale=pcol("ln_g", c))
                    last.then_inc(silu_done, 1)
                    for s in range(RING):
                        ahead("DP", 0, s, WIDTH["DP"][:2])
                    for s in range(RING):
                        ahead("DP", 1, s)
                    with act.Fori(0, 2) as g:
                        for s in range(RING):
                            step("OUT", g, s, mixed[:, 4 * g + s, :])
                    act.wait_ge(added, 1)
                    norm_square(act)
                    act.dma_start(x_keep.rearrange("p (k t) -> p k t", k=KC), x[:, :, :]).then_inc(x_saved, 16)
                    root(act, 2)
                    norm_high(act, 1)
                    act.wait_ge(stored, 16 * 5)
                    with act.Fori(0, 3) as g:
                        for s in range(RING):
                            step("WQ", g, s, q_high[:, 4 * g + s, 0:T], signal=q_high_out)
                    for s in range(RING):
                        step("WQ", 3, s, q_high[:, 12 + s, 0:T], signal=q_high_out, following=WIDTH["KEYS"])
                    for s in range(RING):
                        ahead("KEYS", 0, s)
                    with act.Fori(0, UTAIL) as g:
                        for s in range(RING):
                            step("U", g, s, acts[:, 4 * g + s, :], ACT.Gelu_apprx_tanh)
                    act.wait_ge(selected, TILES)
                    A(routed[:, :, 2, :], routed[:, :, 2, :], ACT.Exp).then_inc(weighed, 1)
                    act.wait_ge(x_saved, 16)
                    with act.Fori(UTAIL, GROUPS["U"] - 2) as g:
                        for s in range(RING):
                            step("U", g, s, acts[:, 4 * g + s, :], ACT.Gelu_apprx_tanh)
                    act.wait_ge(spread, BATCHES)
                    with act.Fori(GROUPS["U"] - 2, GROUPS["U"]) as g:
                        for s in range(RING):
                            step("U", g, s, acts[:, 4 * g + s, :], ACT.Gelu_apprx_tanh)
                    act.wait_ge(spread_out, BATCHES + 2)

                    def c_split(i, slot):
                        A(c_high[:, slot, :], acts[:, i, :], ACT.Copy).then_inc(c_high_out, 1)

                    def v_half_ahead(g, s, half):
                        grp = group("VA", g)
                        s2 = (s + 2) % RING
                        if half == 0:
                            act.wait_ge(landed[s2], 16 * grp + (16 if s < 2 else 32))
                        act.wait_ge(half_done, 2 * number("VA", g, s) + (half + 1))
                        A(w_high[2 * (s % 2) + half][:, :, :], raw[s2][:, 4 * half:4 * half + 4, :], ACT.Copy)\
                            .then_inc(high_done, 1)

                    for i in range(RING):
                        c_split(i, i)
                    with act.Fori(0, PERIODS) as n:
                        for j in range(VA_PERIOD):
                            group_in = 3 * n + j // RING
                            for half, h in enumerate((2 * j + KC // 2, 2 * j + KC // 2 + 1)):
                                v_half_ahead(group_in, j % RING, half)
                                if h % 3 != 1:
                                    i = 2 * (h // 3) + (1 if h % 3 == 0 else 2)
                                    c_split(PERIOD_KEYS * n + i, i % RING)
                    act.wait_ge(spread_out, 2 * BATCHES + 2)
                    with act.Fori(0, GROUPS["VB"] - 1) as g:
                        for s in range(RING):
                            ahead("VB", g, s)
                            c_split(RING * g + (VA_KEYS + s + RING), s)
                    for s in range(RING):
                        ahead("VB", GROUPS["VB"] - 1, s)
                        c_split(s, s)
                    with act.Fori(0, GROUPS["VC"] - 1) as g:
                        for s in range(RING):
                            for half in range(2):
                                act.wait_ge(half_done, 2 * number("VC", g, s) + half + 1)
                                for i in (2 * half, 2 * half + 1):
                                    c_split(4 * RING * g + (4 * s + 4 + i), i)
                                v_half_ahead(g + 9 + 20, s, half)
                    for s in range(RING - 1):
                        for half in range(2):
                            act.wait_ge(half_done, 2 * number("VC", GROUPS["VC"] - 1, s) + half + 1)
                            for i in (2 * half, 2 * half + 1):
                                c_split(4 * RING * (GROUPS["VC"] - 1) + (4 * s + 4 + i), i)
                            if s < 2:
                                v_half_ahead(GROUPS["VC"] - 1 + 9 + 20, s, half)

                @block.vector
                def _(dve):
                    V = nc.vector
                    steps = Steps(dve, v_step)
                    did, settle = steps.did, steps.settle

                    def conv_tap(m, out, bias):
                        e, n = ext[m], CHUNKS[m]
                        col = PCOL["conv_" + m]

                        def tap(j):
                            for c in range(n):
                                w = par[:, bass.ds(j * n + (col + c), 1)]
                                pr = e[:, c, bass.ds(j, TP)]
                                w4 = e[:, c, PAD[m] + TP:row(m)].rearrange("p (b w) -> p b w", b=NB)
                                sa = w4[:, :, bass.ds(j, TS)]
                                o_p, o_s = out[:, c, 0:TP], by_seq(out[:, c, :])
                                if isinstance(j, int):
                                    b = pcol(bias, c) if bias else 0.0
                                    did(V.tensor_scalar(o_p, pr, w, b, ALU.mult, ALU.add))
                                    did(V.tensor_scalar(o_s, sa, w, b, ALU.mult, ALU.add))
                                else:
                                    did(V.scalar_tensor_tensor(o_p, pr, w, o_p, ALU.mult, ALU.add))
                                    did(V.scalar_tensor_tensor(o_s, sa, w, o_s, ALU.mult, ALU.add))

                        return tap

                    def conv(m, out, bias):
                        tap = conv_tap(m, out, bias)
                        tap(0)

                        def body(j):
                            settle()
                            tap(j + 1)
                        steps.loop(CONV[m] - 1, body, 2 * CHUNKS[m])
                        settle()

                    def split(src, name, signal=None):
                        high, low = pair[name]
                        did(V.tensor_copy(high, src))
                        settle()
                        last = V.tensor_tensor(low, src, high.bitcast(F32), ALU.subtract)
                        if signal is None:
                            did(last)
                        else:
                            last.then_inc(signal, 1)

                    V.sem_inc(gates_free, 2)
                    dve.wait_ge(par_in, 16)
                    norm_scale(dve, steps, 0, 1, par[:, PCOL["norm1"]:PCOL["norm1"] + KC])
                    norm_low(dve, 0)
                    dve.wait_ge(padded, 1)
                    dve.wait_ge(ext_loaded, 16 * 5)
                    dve.wait_ge(evacuated, EVAC["B"] + 4)
                    for c in range(CA):
                        src, dst, valid = ext["b"][:, c, :], wins[0], 0
                        for level in range(c + 1):
                            d = 1 << level
                            valid += d
                            did(V.tensor_tensor(dst[:, valid:row("b")], src[:, valid:row("b")],
                                                src[:, valid - d:row("b") - d], ALU.add))
                            settle()
                            src, dst = dst, wins[1] if dst is wins[0] else wins[0]
                        w = 2 << c
                        a = PAD["b"]
                        win = src[:, a + TP:row("b")].rearrange("p (b w) -> p b w", b=NB)[:, :, a:a + TS]
                        did(V.scalar_tensor_tensor(p_b[:, c, 16:TP], src[:, a + 16:a + TP], 1.0 / w,
                                                   ext["b"][:, c, a + 16:a + TP], ALU.mult, ALU.subtract))
                        did(V.scalar_tensor_tensor(by_seq(p_b[:, c, :]), win, 1.0 / w, samples_of(ext["b"], "b", c),
                                                   ALU.mult, ALU.subtract))
                        did(V.tensor_tensor(p_b[:, c, 0:16], src[:, a:a + 16], first_cnt[:, c, :], ALU.mult))
                        settle()
                        did(V.tensor_tensor(p_b[:, c, 0:16], p_b[:, c, 0:16], ext["b"][:, c, a:a + 16], ALU.subtract))
                    settle()
                    split(p_b, "p_b", pooled)

                    did(V.tensor_scalar(lru[:, 0, :], pcol("lam", 0, CC), -1.0, None, ALU.mult))
                    settle()
                    V.tensor_tensor(lru[:, 0, :], lru[:, 0, :], pcol("lam", 0, CC), ALU.max).then_inc(softplus_arg, 1)
                    dve.wait_ge(softplus_exp, 1)
                    did(V.tensor_scalar(lru[:, 2, :], lru[:, 1, :], 2.0, None, ALU.add))
                    settle()
                    did(V.reciprocal(lru[:, 2, :], lru[:, 2, :]))
                    settle()
                    did(V.tensor_tensor(lru[:, 3, :], lru[:, 1, :], lru[:, 2, :], ALU.mult))
                    settle()
                    did(V.tensor_tensor(lru[:, 4, :], lru[:, 3, :], lru[:, 3, :], ALU.mult))
                    settle()
                    did(V.tensor_scalar(lru[:, 5, :], lru[:, 4, :], 2.0 / 17, 2.0 / 15, ALU.mult, ALU.add))
                    for k in (13, 11, 9, 7, 5, 3, 1):
                        settle()
                        did(V.tensor_tensor(lru[:, 5, :], lru[:, 5, :], lru[:, 4, :], ALU.mult))
                        settle()
                        did(V.tensor_scalar(lru[:, 5, :], lru[:, 5, :], 2.0 / k, None, ALU.add))
                    settle()
                    did(V.tensor_tensor(lru[:, 5, :], lru[:, 5, :], lru[:, 3, :], ALU.mult))
                    did(V.tensor_scalar(lru[:, 2, :], pcol("lam", 0, CC), -1.0, 0.0, ALU.mult, ALU.max))
                    settle()
                    did(V.tensor_tensor(lru[:, 5, :], lru[:, 5, :], lru[:, 2, :], ALU.add))
                    settle()
                    V.tensor_scalar(lru[:, 6, :], lru[:, 5, :], -LRU_C, None, ALU.mult)
                    V.tensor_scalar(lru[:, 7, :], lru[:, 5, :], LRU_C, None, ALU.mult).then_inc(softplus_done, 1)

                    dve.wait_ge(evacuated, EVAC["C"] + 8)
                    conv("c", xconv, "conv_c_b")
                    split(xconv, "xconv", c_conv)
                    dve.wait_ge(extra_out, 4)
                    split(y_b, "b", y_ready)

                    dve.wait_ge(lru_exp, 1)
                    did(V.tensor_tensor(ig, ig, xconv, ALU.mult))
                    settle()
                    did(V.tensor_scalar(xconv, rg, 0.5, 0.5, ALU.mult, ALU.add))
                    settle()
                    did(V.reciprocal(xconv, xconv))
                    settle()
                    V.tensor_tensor(rg, rg, xconv, ALU.mult).then_inc(lru_ratio, 1)
                    dve.wait_ge(lru_root, 1)
                    did(V.tensor_tensor(ig, ig, rg, ALU.mult))
                    did(V.tensor_tensor(h0a[:, :, :], by_seq_all(aa)[:, :, :, 0], h0[:, :, :], ALU.mult))
                    settle()
                    did(V.tensor_tensor(by_seq_all(ig)[:, :, :, 0], by_seq_all(ig)[:, :, :, 0], h0a[:, :, :], ALU.add))
                    did(V.memset(by_seq_all(aa)[:, :, :, 0], 0.0))
                    did(V.memset(aa[:, :, 0:1], 0.0))
                    settle()
                    flat = [v.rearrange("p c t -> p (c t)") for v in (xconv, aa, ig)]
                    did(V.tensor_tensor_scan(flat[0], flat[1], flat[2], 0.0, ALU.mult, ALU.add))
                    settle()
                    did(V.tensor_copy(h_last[:, :, 0:1], xconv[:, :, TP - 1:TP]))
                    did(V.tensor_copy(h_last[:, :, 1:1 + NB], by_seq_all(xconv)[:, :, :, TS - 1]))
                    did(V.tensor_tensor(rg, xconv, yg, ALU.mult))
                    settle()
                    split(rg, "c", y_ready)

                    dve.wait_ge(evacuated, EVAC["D"] + 8)
                    did(V.tensor_tensor(prompt_of(ext["d"], "d"), d_val[:, :, 0:TP], d_gate[:, :, 0:TP], ALU.mult))
                    did(V.tensor_tensor(samples_of(ext["d"], "d"), by_seq_all(d_val), by_seq_all(d_gate), ALU.mult))
                    settle()
                    d_tap = conv_tap("d", cd, "conv_d_b")
                    d_tap(0)

                    def d_more(j):
                        settle()
                        d_tap(j + 1)
                    early = CONV["d"] - 1 - 3 * KC
                    steps.loop(early, d_more, 2 * CA)

                    def merge(name, g, s, after):
                        turn = BRANCHES[name][1]
                        c = 2 * g + s // 2
                        dve.wait_ge(half_done, 2 * number(name, g, s) + 2)
                        dve.wait_ge(evacuated, 2 * g + (EVAC[name] + s // 2 + 1))
                        out = acc[:, c, :] if turn == 0 else prod[:, s, :]
                        V.tensor_tensor(out, bank[4 + s][:, 0:T], gates[:, c, :], ALU.mult).then_inc(gates_free, 1)
                        if turn > 0:
                            dve.wait_ge(gates_free, c + (KC * turn + 3))
                            did(V.tensor_tensor(acc[:, c, :], acc[:, c, :], prod[:, s, :], ALU.add))
                        settle()
                        d_tap(c + (after + 1))

                    def merges(name):
                        turn = BRANCHES[name][1]

                        def body(g):
                            for s in (1, 3):
                                merge(name, g, s, early + KC * turn)
                        steps.loop(GROUPS[name], body, 2 * (2 * CA + (turn > 0)))

                    merges("XB")
                    dve.wait_ge(evacuated, EVAC["A"] + 12)
                    gb, gc, xv = ua[:, 0:CA, :], ua[:, CA:2 * CA, :], ua[:, 2 * CA:3 * CA, :]
                    did(V.tensor_tensor(prompt_of(ext["a"], "a"), gc[:, :, 0:TP], xv[:, :, 0:TP], ALU.mult))
                    did(V.tensor_tensor(samples_of(ext["a"], "a"), by_seq_all(gc), by_seq_all(xv), ALU.mult))
                    settle()
                    conv("a", y_a, None)
                    did(V.tensor_tensor(y_a, y_a, gb, ALU.mult))
                    settle()
                    split(y_a, "a", y_ready)
                    merges("XC")
                    merges("XA")
                    settle()
                    V.sem_inc(d_conv, 1)
                    dve.wait_ge(ln_sum1, 1)
                    did(V.tensor_scalar(stat[:, 0, :], bank[4][:, 0:T], 1.0 / W_D, None, ALU.mult))
                    settle()
                    V.tensor_tensor(cd, cd, stat[:, 0:1, :].to_broadcast([P, CA, T]), ALU.subtract).then_inc(ln_centred, 1)
                    dve.wait_ge(ln_sum2, 1)
                    did(V.tensor_scalar(stat[:, 0, :], bank[4][:, 0:T], 1.0 / W_D, EPS, ALU.mult, ALU.add))
                    settle()
                    V.reciprocal(stat[:, 0, :], stat[:, 0, :]).then_inc(inverse, 1)
                    dve.wait_ge(rooted, 2)
                    V.tensor_tensor(cd, cd, stat[:, 1:2, :].to_broadcast([P, CA, T]), ALU.mult).then_inc(ln_scaled, 1)
                    dve.wait_ge(silu_done, 1)
                    split(cd, "d", y_ready)

                    m_high, m_low = pair["merged"]

                    def last_merge(g):
                        for s in range(RING):
                            c = 4 * g + s
                            dve.wait_ge(half_done, 2 * number("DP", g, s) + 2)
                            V.tensor_tensor(prod[:, s, :], bank[4 + s][:, 0:T], gates[:, c, :], ALU.mult)\
                             .then_inc(gates_free, 1)
                            dve.wait_ge(gates_free, c + (3 * KC + 3))
                            did(V.tensor_tensor(prod[:, s, :], prod[:, s, :], acc[:, c, :], ALU.add))
                            settle()
                            did(V.tensor_copy(m_high[:, c, :], prod[:, s, :]))
                            settle()
                            V.tensor_tensor(m_low[:, c, :], prod[:, s, :], m_high[:, c, :].bitcast(F32), ALU.subtract)\
                             .then_inc(chunk_merged, 1)
                    dve.wait_ge(evacuated, EVAC["DG"] + KC)
                    steps.loop(2, last_merge, 2 * RING)

                    dve.wait_ge(evacuated, EVAC["OUT"] + 8)
                    V.tensor_tensor(x[:, :, :], x[:, :, :], mixed, ALU.add).then_inc(added, 1)
                    dve.wait_ge(added, 1)
                    norm_scale(dve, steps, 1, 3, par[:, PCOL["norm2"]:PCOL["norm2"] + KC])
                    norm_low(dve, 1)

                    dve.wait_ge(stored, 16 * 5)
                    did(V.memset(q_high[:, :, T:QCOLS].bitcast(U32), 0))
                    did(V.memset(q_low[:, :, T:QCOLS].bitcast(U32), 0))
                    settle()

                    with dve.Fori(0, 4) as g:
                        for s in range(RING):
                            dve.wait_ge(q_high_out, RING * g + (s + 1))
                            c = 4 * g + s
                            V.tensor_tensor(q_low[:, c, 0:T], bank[s][:, 0:T], q_high[:, c, 0:T].bitcast(F32),
                                            ALU.subtract).then_inc(evacuated, 1)

                    n = 0
                    for s in range(RING):
                        for tt in range(TILES):
                            if tt < TILES - 1:
                                dve.wait_ge(scores_done, 2 * s + tt + 1)
                            else:
                                dve.wait_ge(half_done, 2 * number("KEYS", 0, s) + 2)
                            V.tensor_copy(s_all[:, tt, s * 512:(s + 1) * 512], bank[4 + n % 4][:, :])\
                             .then_inc(scores_out, 1)
                            n += 1
                    dve.wait_ge(scores_out, n)

                    routing = Steps(dve, route_step)
                    did_r, settle_r = routing.did, routing.settle

                    def top16(src, values, where):
                        for r in range(4):
                            did_r(V.max(values(r)[:, 0:8], src(r)))
                        settle_r()
                        for r in range(4):
                            did_r(V.max_index(where(r)[:, 0:8], values(r)[:, 0:8], src(r)))
                        n = src(0).shape[-1]
                        for r in range(4):
                            did_r(V.match_replace(left[:, r, 0:n], values(r)[:, 0:8], src(r), NEG))
                        settle_r()
                        for r in range(4):
                            did_r(V.max(values(r)[:, 8:16], left[:, r, 0:n]))
                        settle_r()
                        for r in range(4):
                            did_r(V.max_index(where(r)[:, 8:16], values(r)[:, 8:16], left[:, r, 0:n]))
                        settle_r()

                    def route(tt):
                        did_r(V.tensor_copy(eq, s_all[:, tt, :]))
                        settle_r()
                        for q in range(HC // 4):
                            top16(lambda r: s_work[:, 4 * q + r, :], lambda r: vals[:, 4 * q + r, :],
                                  lambda r: idxs[:, 4 * q + r, :])
                        did_r(V.tensor_copy(idxf[:, :, :], idxs[:, :, :]))
                        v4 = vals[:, :, :].rearrange("p (h c) k -> p h c k", c=2)
                        first = v4[:, :, 0, :].unsqueeze(3).to_broadcast([P, HEADS, TOPK, TOPK])
                        second = v4[:, :, 1, :].unsqueeze(2).to_broadcast([P, HEADS, TOPK, TOPK])
                        did_r(V.tensor_tensor(cand.rearrange("p h (a b) -> p h a b", a=TOPK), first, second, ALU.add))
                        settle_r()
                        for q in range(HEADS // 4):
                            top16(lambda r: cand[:, 4 * q + r, :], lambda r: best[:, 4 * q + r, :],
                                  lambda r: pos[:, 4 * q + r, :])
                        pf = pos[:, :, :].rearrange("p h k -> p (h k)")
                        did_r(V.tensor_scalar(posab[:, 0, :], pf, 4, None, ALU.logical_shift_right))
                        did_r(V.tensor_scalar(posab[:, 1, :], pf, 15, None, ALU.bitwise_and))
                        settle_r()
                        did_r(V.tensor_copy(posf[:, :, :], posab[:, :, :]))
                        settle_r()
                        i4 = idxf[:, :, :].rearrange("p (h c) k -> p h c k", c=2)
                        e4 = eq.rearrange("p (h k j) -> p h k j", h=HEADS, k=TOPK)
                        e3 = eq.rearrange("p (s j) -> p s j", j=TOPK)
                        for c in range(2):
                            did_r(V.tensor_tensor(e3, posf[:, c, :].unsqueeze(2).to_broadcast([P, HK, TOPK]),
                                                iota16[:, :].unsqueeze(1).to_broadcast([P, HK, TOPK]), ALU.is_equal))
                            settle_r()
                            did_r(V.tensor_tensor(e4, e4, i4[:, :, c, :].unsqueeze(2).to_broadcast([P, HEADS, TOPK, TOPK]),
                                                ALU.mult))
                            settle_r()
                            did_r(V.tensor_reduce(routed[:, tt, c, :], e3, AX.X, ALU.add))
                            settle_r()
                        V.tensor_tensor(routed[:, tt, 2, :].rearrange("p (h k) -> p h k", h=HEADS), best[:, :, :],
                                        best[:, :, 0:1].to_broadcast([P, HEADS, TOPK]), ALU.subtract)\
                         .then_inc(selected, 1)
                        routing.restart()
                    with dve.Fori(0, TILES) as tt:
                        route(tt)
                    dve.wait_ge(weighed, 1)
                    w3 = routed[:, :, 2, :].rearrange("p t (h k) -> p t h k", h=HEADS)
                    d3 = denom[:, :].rearrange("p (t h) -> p t h", t=TILES)
                    did(V.tensor_reduce(d3, w3, AX.X, ALU.add))
                    settle()
                    did(V.reciprocal(denom[:, :], denom[:, :]))
                    settle()
                    V.tensor_tensor(w3, w3, d3.unsqueeze(3).to_broadcast([P, TILES, HEADS, TOPK]), ALU.mult)\
                     .then_inc(gated, 1)
                    dve.wait_ge(turned, 1)
                    for j in range(3):
                        last = V.tensor_copy(selT[:, j, :], bank[4 + j][:, 0:T])
                    last.then_inc(turned_out, 1)
                    dve.wait_ge(turned_out, 1)

                    def onehots_of(stage, c, b):
                        V.tensor_tensor(one1[stage][b][:, :, :], iota[:, :].unsqueeze(1).to_broadcast([P, 4, P]),
                                        selT[:, 0, bass.ds(c, 4)].unsqueeze(2).to_broadcast([P, 4, P]), ALU.is_equal)
                        for t in range(4):
                            last = V.tensor_scalar(one2[stage][b][:, t, :], iota[:, HALF * stage:HALF * (stage + 1)],
                                                   selT[:, 1, bass.ds(c + t, 1)], selT[:, 2, bass.ds(c + t, 1)],
                                                   ALU.is_equal, ALU.mult)
                        last.then_inc(onehots, 1)

                    def weigh(stage, c, b):
                        a = acts[:, HALF * stage:HALF * (stage + 1), bass.ds(c, 4)]
                        V.tensor_tensor(a, a, bank[6 + b][:, 0:4 * HALF].rearrange("p (t i) -> p i t", t=4), ALU.mult)\
                         .then_inc(spread_out, 1)

                    def eight_tokens(stage, n, more=True):
                        for b in range(2):
                            dve.wait_ge(spread, 2 * n + (BATCHES * stage + b + 1))
                            weigh(stage, 8 * n + 4 * b, b)
                            if more:
                                onehots_of(stage, 8 * n + (4 * b + 8), b)

                    V.sem_inc(spread_out, 2)
                    dve.wait_ge(x_saved, 16)
                    dve.wait_ge(evacuated, EVAC["U"] + HALF)
                    onehots_of(0, 0, 0)
                    onehots_of(0, 4, 1)
                    with dve.Fori(0, T // 8 - 1) as n:
                        eight_tokens(0, n)
                    eight_tokens(0, T // 8 - 1, more=False)
                    dve.wait_ge(evacuated, EVAC["U"] + NKEYS)
                    onehots_of(1, 0, 0)
                    onehots_of(1, 4, 1)

                    def low_activations(n, i, slot):
                        dve.wait_ge(c_high_out, n + 1)
                        V.tensor_tensor(c_low[:, slot, :], acts[:, i, :], c_high[:, slot, :].bitcast(F32), ALU.subtract)\
                         .then_inc(c_low_out, 1)

                    def before(j):
                        return (KC * (j + 2) - 1) // VA_CHUNKS + 1

                    def va_gates(n, end=False):
                        for j in range(VA_PERIOD):
                            for i in range(before(j - 1), before(j)):
                                low_activations(PERIOD_KEYS * n + i, PERIOD_KEYS * n + i, i % RING)
                            eight_tokens(1, VA_PERIOD * n + j, more=not (end and j == VA_PERIOD - 1))

                    for i in range(before(-1)):
                        low_activations(i, i, i)
                    with dve.Fori(0, PERIODS - 1) as n:
                        va_gates(n)
                    va_gates(PERIODS - 1, end=True)
                    n = VA_KEYS + before(-1)
                    while n < VA_KEYS + RING:
                        low_activations(n, n, n % RING)
                        n += 1
                    with dve.Fori(1, GROUPS["VB"]) as g:
                        for s in range(RING):
                            low_activations(RING * g + (VA_KEYS + s), RING * g + (VA_KEYS + s), s)
                    with dve.Fori(0, VA_KEYS // RING) as g:
                        for s in range(RING):
                            low_activations(RING * g + (NKEYS + s), RING * g + s, s)
                    dve.wait_ge(half_done, 2 * TOTAL)
                    dve.wait_ge(x_loaded, 16)
                    for c in range(KC):
                        did(V.tensor_tensor(x[:, c, :], x_back[:, c, :], bank[c][:, 0:T], ALU.add))
                    settle()

            nc.sync.sem_clear(range(first_sem.num, last_sem.num + 1))
            nc.all_engine_barrier()

        with nc.Block() as block:
            @block.scalar
            def _(act):
                norm_square(act)
                root(act, 0)
                act.wait_ge(x_raw, KC)
                act.dma_start(y_out.rearrange("p (k t) -> p k t", k=KC), xnf).then_inc(stored, 16)
                act.wait_ge(stored, 16)

            @block.tensor
            def _(pe):
                norm_sum(pe, 0)

            @block.vector
            def _(dve):
                norm_scale(dve, Steps(dve, v_step), 0, 1, final_g[:, :])


def kernel(**inputs):
    import numpy as np
    import concourse.bacc as bacc
    from concourse.bass_utils import run_bass_kernel_spmd

    a = {k: np.asarray(v) for k, v in inputs.items()}
    f32 = np.float32

    def columns(v, j=1):
        v = v.reshape(DEPTH, -1, P)
        return v.transpose(0, 2, 1)

    packs = {"norm1": columns(a["norm1_g"]), "norm2": columns(a["norm2_g"]), "b_gate": columns(a["b_gate"]),
             "conv_a": columns(a["conv_a_w"]), "pool_scale": columns(a["pool_scale"]), "conv_c": columns(a["conv_c_w"]),
             "conv_c_b": columns(a["conv_c_b"]), "ba": columns(a["lru_ba"]), "bi": columns(a["lru_bi"]),
             "lam": columns(a["lru_lambda"]), "conv_d": columns(a["conv_d_w"]), "conv_d_b": columns(a["conv_d_b"]),
             "ln_g": columns(a["ln_d_g"]), "ln_b": columns(a["ln_d_b"])}
    params = np.concatenate([packs[n] for n, _ in PARAMS], axis=2)

    def tiles(w):
        l, d, n = w.shape
        return w.reshape(l, d // P, P, n // P, P).transpose(0, 3, 2, 1, 4).reshape(l, n // P, P, d)

    wt = tiles(a["w_in"])
    off_b, off_c, off_d, off_g = 12, 16, 32, 40
    order = [off_b + i for i in range(4)] + [off_c + i for i in range(16)] + [off_d + i for i in range(8)]
    order += list(range(12)) + [off_g + i for i in range(4 * KC)]
    w_in = wt[:, order]

    def ext_rows(s, m):
        v = s.reshape(DEPTH, NB, PAD[m], CHUNKS[m], P).transpose(0, 4, 3, 1, 2)
        out = np.zeros((DEPTH, P, CHUNKS[m], NB, PAD[m] + TS), f32)
        out[..., :PAD[m]] = v
        return out.reshape(DEPTH, P, CHUNKS[m], NB * (PAD[m] + TS))

    v = a["peer_v"].reshape(DEPTH, NKEYS, NKEYS, KC, P).transpose(0, 2, 3, 1, 4)

    def v_tiles(blocks):
        return blocks.reshape(DEPTH, -1, KC, P, P).transpose(0, 1, 3, 2, 4).reshape(DEPTH, -1, P, DM)

    xt = np.concatenate([a["x_prompt"].reshape(TP, DM), a["x_sample"].reshape(NB * TS, DM)])
    arrays = {
        "x_in": xt.reshape(T, KC, P).transpose(2, 1, 0).reshape(P, KC * T),
        "params_in": params,
        "final_in": a["final_g"].reshape(KC, P).T,
        "pool_first": np.broadcast_to(np.array([[1.0 / min(t + 1, 2 << g) for t in range(16)] for g in range(CA)], f32),
                                      (P, CA, 16)),
        "ext_a": ext_rows(a["state_conv_a"], "a"), "ext_b": ext_rows(a["state_pool"], "b"),
        "ext_c": ext_rows(a["state_conv_c"], "c"), "ext_d": ext_rows(a["state_conv_d"], "d"),
        "h0_in": a["state_lru_h"].reshape(DEPTH, NB, CC, P).transpose(0, 3, 2, 1),
        "w_in_t": w_in,
        "w_pool": a["pool_w"].transpose(0, 2, 1, 3).reshape(DEPTH, P, CA * P),
        "w_lru": np.stack([a["lru_wa"].transpose(0, 2, 1, 3), a["lru_wi"].transpose(0, 2, 1, 3)], 1)
                   .reshape(DEPTH, 2, P, CC * P),
        "w_ab": np.stack([tiles(a["w_pa"]), tiles(a["w_pb"])], axis=1),
        "w_c": tiles(a["w_pc"]), "w_d": tiles(a["w_pd"]), "w_out_t": tiles(a["w_out"]), "w_q": tiles(a["peer_wq"]),
        "w_keys": a["peer_keys"].reshape(DEPTH, 4, 4, NKEYS, P).transpose(0, 1, 4, 2, 3).reshape(DEPTH, 4, P, 4 * P),
        "w_u": a["peer_u"].reshape(DEPTH, NKEYS, NKEYS, KC, P).transpose(0, 2, 4, 3, 1).reshape(DEPTH, NKEYS, P, DM),
        "w_v": np.concatenate([v_tiles(v[:, :VA_KEYS, :VA_CHUNKS]), v_tiles(v[:, VA_KEYS:]),
                               v_tiles(v[:, :VA_KEYS, VA_CHUNKS:])], axis=1),
    }
    arrays = {k: np.ascontiguousarray(v) for k, v in arrays.items()}

    nc = bacc.Bacc("TRN2", target_bir_lowering=False, num_devices=1)

    def dram(name, shape, kind):
        return nc.dram_tensor(name, shape, F32, kind=kind).ap()

    i = {k: dram(k, v.shape, "ExternalInput") for k, v in arrays.items()}
    y = dram("y_out", (P, KC * T), "ExternalOutput")
    ext_out = {m: dram(f"ext_out_{m}", (DEPTH, P, CHUNKS[m], tail(m)), "ExternalOutput") for m in "abcd"}
    h_out = dram("h_out", (DEPTH, P, CC, 1 + NB), "ExternalOutput")
    build(nc, i["x_in"], i["params_in"], i["final_in"], i["pool_first"], {m: i[f"ext_{m}"] for m in "abcd"}, i["h0_in"],
          i["w_in_t"], i["w_pool"], i["w_lru"], i["w_ab"], i["w_c"], i["w_d"], i["w_out_t"], i["w_q"], i["w_keys"],
          i["w_u"], i["w_v"], nc.dram_tensor("x_keep", (P, KC * T), F32).ap(), y, ext_out, h_out)
    r = run_bass_kernel_spmd(nc, [arrays], core_ids=[0]).results[0]

    yt = r["y_out"].reshape(P, KC, T).transpose(2, 1, 0).reshape(T, DM)
    outs = [yt[:TP].reshape(1, TP, DM), yt[TP:].reshape(NB, TS, DM)]

    def states(m):
        e = r[f"ext_out_{m}"]
        p = e[..., :PAD[m]].transpose(0, 3, 2, 1).reshape(DEPTH, 1, PAD[m], CHUNKS[m] * P)
        s = e[..., PAD[m]:].reshape(DEPTH, P, CHUNKS[m], NB, PAD[m] + TS)[..., TS:]
        return [p, s.transpose(0, 3, 4, 2, 1).reshape(DEPTH, NB, PAD[m], CHUNKS[m] * P)]

    h = r["h_out"].transpose(0, 3, 2, 1).reshape(DEPTH, 1 + NB, DM)
    outs += states("a") + states("b") + states("c") + [h[:, :1], h[:, 1:]] + states("d")
    return tuple(np.ascontiguousarray(o) for o in outs)
```
